# Optimizing a Trainium2 kernel written in Bass

```python
import jax, jax.numpy as jnp
from jax import lax
import numpy as np

D_MODEL = 1024
BATCH = 1
SEQ = 256
DEPTH = 2
DEC_BATCH = 1
DEC_SEQ = 64
PAST_LEN = 512

CHUNK = 64
POOL_WINDOWS = (2, 4, 8, 16)
N_POOL_GROUPS = len(POOL_WINDOWS)
POOL_GW = D_MODEL // N_POOL_GROUPS
POOL_BUF = max(POOL_WINDOWS) - 1
WINDOW = 128
N_BACK = WINDOW // CHUNK
HEAD_DIM = 64
N_HEADS = D_MODEL // HEAD_DIM
N_KV_HEADS = 4
GROUP = N_HEADS // N_KV_HEADS
D_FF = 7 * D_MODEL // 2
N_EXPERTS = 8
TOP_K = 2
PLE_DIM = 256
EPS = 1e-6
N_A = DEPTH // 2
N_B = DEPTH - N_A
N_DENSE = (DEPTH + 1) // 2
N_MOE = DEPTH // 2
NEG = -1e30

kernel_name = 'yoco_pool_swa_sink_stream_step'

def _rmsnorm(x, g):
    xf = x.astype(jnp.float32)
    y = xf * lax.rsqrt(jnp.mean(xf * xf, axis=-1, keepdims=True) + EPS)
    return (y * g.astype(jnp.float32)).astype(x.dtype)

def _kv_buf_len():
    return min(N_BACK * CHUNK, PAST_LEN)

def _pool_mixer(h, prev, mask, w_pool, scale):
    b, t, _ = h.shape
    p = prev.shape[1]
    cat = jnp.concatenate([prev.astype(h.dtype), h], axis=1).astype(jnp.float32)
    cs = jnp.pad(jnp.cumsum(cat, axis=1), ((0, 0), (1, 0), (0, 0)))
    cm = jnp.pad(jnp.cumsum(mask.astype(jnp.float32)), (1, 0))
    end = cs[:, p + 1:p + 1 + t]
    cnt_end = cm[p + 1:p + 1 + t]
    means = []
    for gi, w in enumerate(POOL_WINDOWS):
        sl = slice(gi * POOL_GW, (gi + 1) * POOL_GW)
        s = end[:, :, sl] - cs[:, p + 1 - w:p + 1 - w + t, sl]
        c = cnt_end - cm[p + 1 - w:p + 1 - w + t]
        means.append(s / c[None, :, None])
    diff = jnp.stack(means, axis=2) - h.astype(jnp.float32).reshape(b, t, N_POOL_GROUPS, POOL_GW)
    y = jnp.einsum('btgc,gce->btge', diff.astype(h.dtype), w_pool).reshape(b, t, D_MODEL)
    return y * scale

def _sink_softmax(s, sink):
    sink_b = jnp.broadcast_to(sink.astype(jnp.float32), s.shape[:-1] + (1,))
    pr = jax.nn.softmax(jnp.concatenate([s, sink_b], axis=-1), axis=-1)
    return pr[..., :-1]

def _swa_prompt(q, k, v, sink):
    b, s = q.shape[0], q.shape[1]
    nc = s // CHUNK
    pad = ((0, 0), (N_BACK * CHUNK, 0), (0, 0), (0, 0))
    kp = jnp.pad(k, pad).reshape(b, nc + N_BACK, CHUNK, N_KV_HEADS, HEAD_DIM)
    vp = jnp.pad(v, pad).reshape(b, nc + N_BACK, CHUNK, N_KV_HEADS, HEAD_DIM)
    kb = jnp.concatenate([kp[:, j:j + nc] for j in range(N_BACK + 1)], axis=2)
    vb = jnp.concatenate([vp[:, j:j + nc] for j in range(N_BACK + 1)], axis=2)
    key_chunk = jnp.arange(nc)[:, None] - N_BACK + jnp.arange(N_BACK + 1)[None, :]
    valid = jnp.repeat(key_chunk >= 0, CHUNK, axis=1)
    qc = q.reshape(b, nc, CHUNK, N_KV_HEADS, GROUP, HEAD_DIM)
    sc = jnp.einsum('bnqkgd,bnskd->bnkgqs', qc, kb,
                    preferred_element_type=jnp.float32) * (HEAD_DIM ** -0.5)
    sc = jnp.where(valid[None, :, None, None, None, :], sc, NEG)
    pr = _sink_softmax(sc, sink.reshape(N_KV_HEADS, GROUP)[None, None, :, :, None, None])
    o = jnp.einsum('bnkgqs,bnskd->bnqkgd', pr.astype(vb.dtype), vb)
    return o.reshape(b, s, N_HEADS * HEAD_DIM)

def _swa_sample(q, kk, vv, sink):
    b, t = q.shape[0], q.shape[1]
    sc = jnp.einsum('btkgd,bskd->bkgts', q, kk,
                    preferred_element_type=jnp.float32) * (HEAD_DIM ** -0.5)
    pr = _sink_softmax(sc, sink.reshape(N_KV_HEADS, GROUP)[None, :, :, None, None])
    o = jnp.einsum('bkgts,bskd->btkgd', pr.astype(vv.dtype), vv)
    return o.reshape(b, t, N_HEADS * HEAD_DIM)

def _swiglu(h, w1, w3, w2):
    return (jax.nn.silu(h @ w1) * (h @ w3)) @ w2

def _moe(h, w_router, b_router, w1, w3, w2):
    logits = jnp.einsum('btd,de->bte', h, w_router,
                        preferred_element_type=jnp.float32) + b_router.astype(jnp.float32)
    vals, idx = lax.top_k(logits, TOP_K)
    gates = jax.nn.softmax(vals, axis=-1)
    gate_full = jnp.sum(jax.nn.one_hot(idx, N_EXPERTS, dtype=jnp.float32) * gates[..., None], axis=-2)
    y = jnp.zeros_like(h)
    for e in range(N_EXPERTS):
        y = y + gate_full[..., e:e + 1].astype(h.dtype) * _swiglu(h, w1[e], w3[e], w2[e])
    return y

def _trunk(x, p, pool_prev, pool_mask, cache_k, cache_v,
           g_mix, g_ffn, g_ple, g_kv, g_final, w_pool, pool_scale,
           w_q, b_q, w_k, b_k, w_v, b_v, w_o, sinks,
           w1_dense, w3_dense, w2_dense, w_router, b_router, w1_moe, w3_moe, w2_moe,
           w_ple_proj, w_ple_gate):
    prompt = cache_k is None
    b, t, _ = x.shape
    kv_buf = _kv_buf_len()
    new_pool = []
    kk = vv = new_k = new_v = None
    for i in range(DEPTH):
        h = _rmsnorm(x, g_mix[i])
        if i < N_A:
            x = x + _pool_mixer(h, pool_prev[i], pool_mask, w_pool[i], pool_scale[i])
            new_pool.append(jnp.concatenate([pool_prev[i].astype(h.dtype), h], axis=1)[:, -POOL_BUF:])
        else:
            j = i - N_A
            q = (h @ w_q[j] + b_q[j]).reshape(b, t, N_KV_HEADS, GROUP, HEAD_DIM)
            if prompt:
                o = _swa_prompt(q, kk, vv, sinks[j])
            else:
                o = _swa_sample(q, kk, vv, sinks[j])
            x = x + o @ w_o[j]
        h = _rmsnorm(x, g_ffn[i])
        if i % 2 == 0:
            x = x + _swiglu(h, w1_dense[i // 2], w3_dense[i // 2], w2_dense[i // 2])
        else:
            x = x + _moe(h, w_router[i // 2], b_router[i // 2],
                         w1_moe[i // 2], w3_moe[i // 2], w2_moe[i // 2])
        e_ple = p[i].astype(x.dtype) @ w_ple_proj[i]
        gate = jax.nn.sigmoid(_rmsnorm(x, g_ple[i]) @ w_ple_gate[i])
        x = x + gate * e_ple
        if i == N_A - 1:
            kv_in = _rmsnorm(x, g_kv)
            k = (kv_in @ w_k + b_k).reshape(b, t, N_KV_HEADS, HEAD_DIM)
            v = (kv_in @ w_v + b_v).reshape(b, t, N_KV_HEADS, HEAD_DIM)
            if prompt:
                kk, vv = k, v
            else:
                kk = jnp.concatenate([cache_k.astype(k.dtype), k], axis=1)
                vv = jnp.concatenate([cache_v.astype(v.dtype), v], axis=1)
            new_k = kk[:, -kv_buf:]
            new_v = vv[:, -kv_buf:]
    return _rmsnorm(x, g_final), jnp.stack(new_pool, axis=0), new_k, new_v

def setup_inputs(seed: int = 0) -> dict:
    key = jax.random.key(seed)
    ks = iter(jax.random.split(key, 40))
    f32 = jnp.float32

    def nrm(shape, scale=1.0):
        return jax.random.normal(next(ks), shape, f32) * scale

    kv_buf = _kv_buf_len()
    kvw = N_KV_HEADS * HEAD_DIM
    qw = N_HEADS * HEAD_DIM
    return {
        'x_prompt': nrm((BATCH, SEQ, D_MODEL)),
        'x_sample': nrm((DEC_BATCH, DEC_SEQ, D_MODEL)),
        'state_pool': nrm((N_A, DEC_BATCH, POOL_BUF, D_MODEL)),
        'cache_k': nrm((DEC_BATCH, kv_buf, N_KV_HEADS, HEAD_DIM)),
        'cache_v': nrm((DEC_BATCH, kv_buf, N_KV_HEADS, HEAD_DIM)),
        'p_prompt': nrm((DEPTH, BATCH, SEQ, PLE_DIM)),
        'p_sample': nrm((DEPTH, DEC_BATCH, DEC_SEQ, PLE_DIM)),
        'g_mix': 1.0 + nrm((DEPTH, D_MODEL), 0.05),
        'g_ffn': 1.0 + nrm((DEPTH, D_MODEL), 0.05),
        'g_ple': 1.0 + nrm((DEPTH, D_MODEL), 0.05),
        'g_kv': 1.0 + nrm((D_MODEL,), 0.05),
        'g_final': 1.0 + nrm((D_MODEL,), 0.05),
        'w_pool': nrm((N_A, N_POOL_GROUPS, POOL_GW, POOL_GW), POOL_GW ** -0.5),
        'pool_scale': 1.0 + nrm((N_A, D_MODEL), 0.1),
        'w_q': nrm((N_B, D_MODEL, qw), D_MODEL ** -0.5),
        'b_q': nrm((N_B, qw), 0.02),
        'w_k': nrm((D_MODEL, kvw), D_MODEL ** -0.5),
        'b_k': nrm((kvw,), 0.02),
        'w_v': nrm((D_MODEL, kvw), D_MODEL ** -0.5),
        'b_v': nrm((kvw,), 0.02),
        'w_o': nrm((N_B, qw, D_MODEL), qw ** -0.5),
        'sinks': nrm((N_B, N_HEADS), 0.5),
        'w1_dense': nrm((N_DENSE, D_MODEL, D_FF), D_MODEL ** -0.5),
        'w3_dense': nrm((N_DENSE, D_MODEL, D_FF), D_MODEL ** -0.5),
        'w2_dense': nrm((N_DENSE, D_FF, D_MODEL), D_FF ** -0.5),
        'w_router': nrm((N_MOE, D_MODEL, N_EXPERTS), D_MODEL ** -0.5),
        'b_router': nrm((N_MOE, N_EXPERTS), 0.01),
        'w1_moe': nrm((N_MOE, N_EXPERTS, D_MODEL, D_FF), D_MODEL ** -0.5),
        'w3_moe': nrm((N_MOE, N_EXPERTS, D_MODEL, D_FF), D_MODEL ** -0.5),
        'w2_moe': nrm((N_MOE, N_EXPERTS, D_FF, D_MODEL), D_FF ** -0.5),
        'w_ple_proj': nrm((DEPTH, PLE_DIM, D_MODEL), PLE_DIM ** -0.5),
        'w_ple_gate': nrm((DEPTH, D_MODEL, D_MODEL), D_MODEL ** -0.5),
    }

def reference(x_prompt, x_sample, state_pool, cache_k, cache_v, p_prompt, p_sample,
              g_mix, g_ffn, g_ple, g_kv, g_final, w_pool, pool_scale,
              w_q, b_q, w_k, b_k, w_v, b_v, w_o, sinks,
              w1_dense, w3_dense, w2_dense, w_router, b_router, w1_moe, w3_moe, w2_moe,
              w_ple_proj, w_ple_gate):
    weights = (g_mix, g_ffn, g_ple, g_kv, g_final, w_pool, pool_scale,
               w_q, b_q, w_k, b_k, w_v, b_v, w_o, sinks,
               w1_dense, w3_dense, w2_dense, w_router, b_router, w1_moe, w3_moe, w2_moe,
               w_ple_proj, w_ple_gate)
    bp, tp = x_prompt.shape[0], x_prompt.shape[1]
    ts = x_sample.shape[1]
    prev_p = jnp.zeros((N_A, bp, POOL_BUF, D_MODEL), x_prompt.dtype)
    mask_p = jnp.concatenate([jnp.zeros((POOL_BUF,), jnp.float32), jnp.ones((tp,), jnp.float32)])
    y_prompt, pool_p, k_p, v_p = _trunk(x_prompt, p_prompt, prev_p, mask_p, None, None, *weights)
    mask_s = jnp.ones((POOL_BUF + ts,), jnp.float32)
    y_sample, pool_s, k_s, v_s = _trunk(x_sample, p_sample, state_pool, mask_s, cache_k, cache_v, *weights)
    return (y_prompt, y_sample, pool_p, pool_s, k_p, v_p, k_s, v_s)


_drawn_inputs = setup_inputs


def setup_inputs(seed=0):
    import zlib

    import numpy as np

    out = dict(_drawn_inputs(seed))
    spreads = {}
    factors = {'g_ple': 2.957, 'b_q': 8.0, 'b_k': 3.053, 'sinks': 34.518, 'b_router': 4.858, 'b_v': 2.674}
    for name, (base, spread) in spreads.items():
        noise = np.random.default_rng([zlib.crc32(name.encode()), seed]).standard_normal(out[name].shape)
        drawn = base * np.exp(spread * noise) if base else spread * noise
        out[name] = __import__('jax').numpy.asarray(drawn.astype(out[name].dtype))
    for name, factor in factors.items():
        out[name] = (out[name] * factor).astype(out[name].dtype)
    return out
```

```python
import concourse.bass as bass
from concourse import mybir
from contextlib import ExitStack

F32 = mybir.dt.float32
BF16 = mybir.dt.bfloat16
I32 = mybir.dt.int32
U32 = mybir.dt.uint32
ALU = mybir.AluOpType
ACT = mybir.ActivationFunctionType
AX = mybir.AxisListType

P = 128
D, TP, TS = 1024, 256, 64
T = TP + TS
KC = D // P
FF = 3584
FC = FF // P
NE = 8
HIST = 15
PADP, PADS = HIST, HIST + TP + HIST
LCAT = PADS + TS
PLE = 256
NEG = -1e30
EPS = 1e-6
G_MIX0, G_FFN0, G_PLE0, G_KV, G_MIX1, G_FFN1, G_PLE1, G_FIN, POOL_SC, B_Q, B_K = range(11)
NVEC = 11

SLOT, NSLOT = 4096, 7
RING = SLOT * NSLOT
QUART = RING // 4
NBK = 7
SEQ = [("g", 0), ("u", 0)]
for _b in range(1, NBK):
    SEQ += [("g", _b), ("u", _b), ("d", _b - 1)]
SEQ += [("d", NBK - 1)]
NU = len(SEQ)
POS = {s: n for n, s in enumerate(SEQ)}


def build(nc, A):
    ctx = ExitStack()
    with ctx:
        def sb(name, shape, dt=F32):
            return ctx.enter_context(nc.sbuf_tensor("s_" + name, shape, dt))

        def sem(name):
            return ctx.enter_context(nc.semaphore(name))

        PS = ctx.enter_context(nc.psum_tensor("PS", [P, 8, 512], F32))
        ring = sb("ring", [P, RING])
        G = sb("G", [P, FC * T])
        xT = sb("xT", [P, KC, T])
        hT = sb("hT", [P, KC, T])
        sq = sb("sq", [P, KC * T])
        eple = sb("eple", [P, KC * T])
        side = sb("side", [P, 2048])
        pT = sb("pT", [P, 2, T])
        vec = sb("vec", [P, NVEC, KC])
        std = sb("std", [P, T])
        rstd = sb("rstd", [P, T])
        eps = sb("eps", [P, 1])
        ones = sb("ones", [P, P])
        ident = sb("ident", [P, P])
        tri = sb("tri", [P, P])
        identb = sb("identb", [P, P], BF16)
        mask = sb("mask", [P, 384], BF16)
        iota_i = sb("iota_i", [P, 16], I32)
        iota = sb("iota", [P, T])
        wr = sb("wr", [P, KC, NE])
        rows = sb("rows", [1, 256 + NE])
        sinks = sb("sinks", [P, 40])
        st = sb("st", [P, 64])
        lg = sb("lg", [P, 3, NE])
        top = sb("top", [P, 3, NE])
        topi = sb("topi", [P, 3, NE], U32)
        rt = sb("rt", [P, 3, 4])
        oh = sb("oh", [P, 3, NE])
        gate = sb("gate", [P, 3, NE])
        sel = sb("sel", [P, 3, NE])
        posm = sb("posm", [P, 3, NE])
        tg = sb("tg", [P, 3, 2])
        si = sb("si", [P, 2])
        cnt = sb("cnt", [1, 4])
        extra = sb("extra", [1, 1], I32)

        def view(t, a, n, k=None):
            v = t[:, a:a + n]
            return v if k is None else v.rearrange("p (k n) -> p k n", k=k)

        sq3 = view(sq, 0, KC * T, KC)
        ep3 = view(eple, 0, KC * T, KC)
        L8 = KC * LCAT
        hcat, sA, sB = view(G, 0, L8, KC), view(G, L8, L8, KC), view(G, 2 * L8, L8, KC)
        invc = view(eple, 0, 4 * T, 4)
        wpool = view(side, 0, 2048, 8)
        sg = view(eple, 4 * T, 2 * T, 2)
        guT = view(G, 0, FC * T, FC)
        proj = view(side, 0, 2048, 2)
        sig, gtm = view(G, 0, 2 * T, 2), view(G, 2 * T, 2 * T, 2)
        wgate = view(ring, 0, 2 * SLOT, KC)
        kvT, qT = view(G, 0, KC * T, KC), view(G, KC * T, KC * T, KC)
        oT = kvT
        NKEY = TP + 128 + TS
        kTt = view(G, 2 * KC * T, 2 * NKEY, 2)
        vv = view(G, 2 * KC * T + 2 * NKEY, 1024, 4)
        pb0 = 2 * KC * T + 2 * NKEY + 1024
        pp = view(G, pb0, 4 * 384, 4)
        psm = view(G, pb0 + 4 * 384, 2 * 192, 2)
        pTh = view(sq, 0, 4 * 384, 4)
        pTs = view(sq, 4 * 384, 512, 4)
        wk, wv = view(ring, 2 * SLOT, 2048, KC), view(ring, 2 * SLOT + 2048, 2048, KC)
        wq, wo = view(ring, 3 * SLOT, 2 * SLOT, KC), view(ring, 5 * SLOT, 2 * SLOT, KC)
        hrow = view(G, 0, 3 * D, 3)
        xg = view(G, 3072, KC * P, KC)
        guTm = view(G, 4096, 1024, 8)
        sgm, gum = view(G, 5120, 1024, 2), view(G, 6144, 1024, 2)
        ysb = view(G, 7168, 1024)
        Pm = view(G, 8192, 384, 3)
        PT = view(G, 8576, T)
        g1024 = ring

        def slot(n):
            return view(g1024, (n % NSLOT) * SLOT, SLOT)

        x_loaded, vec_loaded, small_loaded, pool_loaded = sem("x_loaded"), sem("vec_loaded"), sem("small_loaded"), sem("pool_loaded")
        hist_loaded = sem("hist_loaded")
        quart_loaded = [sem(f"quart_loaded{q}") for q in range(4)]
        proj_loaded, p_loaded, gate_loaded = sem("proj_loaded"), sem("p_loaded"), sem("gate_loaded")
        kv_loaded, wq_loaded, wo_loaded, cache_loaded = sem("kv_loaded"), sem("wq_loaded"), sem("wo_loaded"), sem("cache_loaded")
        slot_loaded = [sem(f"slot_loaded{s}") for s in range(NSLOT)]
        pool_stored, kv_stored, y_stored = sem("pool_stored"), sem("kv_stored"), sem("y_stored")
        consts, hzero = sem("consts"), sem("hzero")
        sq_ready, stat_done, std_ready, h_ready, x_ready = sem("sq_ready"), sem("stat_done"), sem("std_ready"), sem("h_ready"), sem("x_ready")
        chain = sem("chain")
        hcat_ready, diff_ready, pool_done = sem("hcat_ready"), sem("diff_ready"), sem("pool_done")
        g_done, u_done, silu_done, gu_ready, down_done = sem("g_done"), sem("u_done"), sem("silu_done"), sem("gu_ready"), sem("down_done")
        eple_mm, eple_ready, gate_done, sig_ready = sem("eple_mm"), sem("eple_ready"), sem("gate_done"), sem("sig_ready")
        k_done, k_ready, v_done, v_ready, q_done, q_ready = (sem(n) for n in ("k_done", "k_ready", "v_done", "v_ready", "q_done", "q_ready"))
        score_done, max_ready, exp_done, p_ready = sem("score_done"), sem("max_ready"), sem("exp_done"), sem("p_ready")
        pT_done, pT_ready, pv_done, o_ready, oproj_done = sem("pT_done"), sem("pT_ready"), sem("pv_done"), sem("o_ready"), sem("oproj_done")
        lg_done, lg_ready, top_ready, gexp_ready, sel_ready, pos_done, routed = (sem(n) for n in (
            "lg_done", "lg_ready", "top_ready", "gexp_ready", "sel_ready", "pos_done", "routed"))
        hrow_done, hrow_ready = sem("hrow_done"), sem("hrow_ready")
        unit_done, msilu_done, gum_ready, t_done, t_ready = sem("unit_done"), sem("msilu_done"), sem("gum_ready"), sem("t_done"), sem("t_ready")
        P_ready, gath_done, xg_ready, slots_done, si_ready, PT_ready = (sem(n) for n in (
            "P_ready", "gath_done", "xg_ready", "slots_done", "si_ready", "PT_ready"))
        scat_done, y_added, y_ready, stepped = sem("scat_done"), sem("y_added"), sem("y_ready"), sem("stepped")

        block = ctx.enter_context(nc.Block())

        def load_unit(sp, e, n):
            kind, b = SEQ[n]
            one = bass.ds(e, 1)
            if kind == "d":
                src = A["w2_moe"][one, 512 * b:512 * b + 512, :].rearrange("a (f p) n -> p (a f) n", p=P)
                dst = slot(n).rearrange("p (f n) -> p f n", f=4)
            else:
                w = A["w1_moe" if kind == "g" else "w3_moe"]
                src = w[one, :, 512 * b:512 * b + 512].rearrange("a (k p) n -> p (a k) n", p=P)
                dst = slot(n).rearrange("p (k n) -> p k n", k=KC)
            sp.dma_start(dst, src).then_inc(slot_loaded[n % NSLOT], 16)

        @block.sync
        def _(sp):
            sp.dma_start(vec[:, :, :], A["vec"]).then_inc(vec_loaded, 16)
            sp.dma_start(xT[:, :, :], A["xT"].rearrange("(k p) t -> p k t", p=P)).then_inc(x_loaded, 16)
            sp.dma_start(wpool, A["w_pool"].rearrange("g (c p) n -> p (g c) n", p=P)).then_inc(pool_loaded, 16)

            def load_up(b):
                for w, q in (("w1_dense", 2 * (b % 2)), ("w3_dense", 2 * (b % 2) + 1)):
                    sp.dma_start(view(ring, q * QUART, QUART, KC),
                                 A[w][:, 896 * b:896 * b + 896].rearrange("(k p) n -> p k n", p=P)).then_inc(quart_loaded[q], 16)

            for b in range(4):
                if b >= 2:
                    sp.wait_ge(u_done, 7 * (b - 1))
                load_up(b)
            sp.wait_ge(pool_done, 8)
            sp.dma_start(proj, A["w_ple_proj"][0].rearrange("(k p) n -> p k n", p=P)).then_inc(proj_loaded, 16)
            for dp in range(4):
                sp.wait_ge(u_done, 7 * (3 + dp // 2))
                sp.dma_start(view(ring, dp * QUART, QUART, FC),
                             A["w2_dense"][:, 256 * dp:256 * dp + 256].rearrange("(f p) n -> p f n", p=P)).then_inc(quart_loaded[dp], 16)
            sp.wait_ge(down_done, 4)
            sp.dma_start(wgate, A["w_ple_gate"][0].rearrange("(k p) n -> p k n", p=P)).then_inc(gate_loaded, 16)
            sp.dma_start(wk, A["w_k"].rearrange("(k p) n -> p k n", p=P)).then_inc(kv_loaded, 16)
            sp.dma_start(wv, A["w_v"].rearrange("(k p) n -> p k n", p=P)).then_inc(kv_loaded, 16)
            sp.wait_ge(down_done, 6)
            sp.dma_start(wq, A["w_q"].rearrange("(k p) n -> p k n", p=P)).then_inc(wq_loaded, 16)
            sp.wait_ge(down_done, 8)
            sp.dma_start(wo, A["w_o"].rearrange("(k p) n -> p k n", p=P)).then_inc(wo_loaded, 16)
            sp.wait_ge(eple_mm, 8)
            sp.dma_start(proj, A["w_ple_proj"][1].rearrange("(k p) n -> p k n", p=P)).then_inc(proj_loaded, 16)
            sp.dma_start(pT[:, :, :], A["pT"][1].rearrange("(k p) t -> p k t", p=P)).then_inc(p_loaded, 16)
            sp.wait_ge(gate_done, 8)
            load_unit(sp, 0, 0)
            load_unit(sp, 0, 1)
            sp.wait_ge(k_done, 2)
            sp.wait_ge(v_done, 3)
            load_unit(sp, 0, 2)
            sp.wait_ge(q_done, 8)
            load_unit(sp, 0, 3)
            load_unit(sp, 0, 4)
            sp.wait_ge(k_ready, 2)
            sp.wait_ge(v_ready, 4)
            sp.wait_ge(cache_loaded, 32)
            ko = A["kT_prompt"].rearrange("(a p) t -> p a t", p=P)
            sp.dma_start(ko, kTt[:, :, TP - 128:TP]).then_inc(kv_stored, 16)
            sp.dma_start(A["kT_sample"].rearrange("(a p) t -> p a t", p=P), kTt[:, :, TP + 64:TP + 192]).then_inc(kv_stored, 16)
            sp.dma_start(A["v_prompt"], vv[:, 1, :]).then_inc(kv_stored, 16)
            sp.dma_start(A["v_sample"][0:64], vv[64:128, 3, :]).then_inc(kv_stored, 16)
            sp.dma_start(A["v_sample"][64:128], vv[0:64, 2, :]).then_inc(kv_stored, 16)
            sp.wait_ge(oproj_done, 8)
            load_unit(sp, 0, 5)
            load_unit(sp, 0, 6)
            sp.wait_ge(routed, 1)
            n = sp.value_load(extra[0:1, 0:1], min_val=0, max_val=2)
            with sp.Fori(0, n * NE + (NE - 1)) as i:
                for u in range(NSLOT, NU):
                    sp.wait_ge(unit_done, i * NU + (u - NSLOT + 1))
                    load_unit(sp, i % NE, u)
                for u in range(NSLOT):
                    sp.wait_ge(unit_done, i * NU + (NU + u - NSLOT + 1))
                    load_unit(sp, (i + 1) % NE, u)
            for u in range(NSLOT, NU):
                sp.wait_ge(unit_done, n * (NE * NU) + (NE * NU + u - NSLOT + 1 - NU))
                load_unit(sp, NE - 1, u)
            sp.wait_ge(unit_done, n * (NE * NU) + (NE * NU + 16 - NU))
            sp.dma_start(wgate, A["w_ple_gate"][1].rearrange("(k p) n -> p k n", p=P)).then_inc(gate_loaded, 16)
            yo = A["yT"].rearrange("(k p) t -> p k t", p=P)
            for c in range(0, KC, 2):
                sp.wait_ge(h_ready, 48 + c + 2)
                sp.dma_start(yo[:, c:c + 2, :], hT[:, c:c + 2, :]).then_inc(y_stored, 16)
            sp.wait_ge(pool_stored, 32)
            sp.wait_ge(kv_stored, 80)
            sp.wait_ge(y_stored, 64)

        @block.gpsimd
        def _(pool):
            pool.memset(ones[:, :], 1.0).then_inc(consts, 1)
            pool.memset(eps[:, :], EPS).then_inc(consts, 1)
            pool.memset(hcat[:, :, 0:HIST], 0.0).then_inc(hzero, 1)
            pool.dma_start(hcat[:, :, PADS - HIST:PADS], A["histT"].rearrange("(k p) t -> p k t", p=P)).then_inc(hist_loaded, 16)
            pool.iota(iota_i[:, :], pattern=[[1, 16]], base=1, channel_multiplier=0).then_inc(consts, 1)
            pool.iota(iota[:, :], pattern=[[1, T]], base=0, channel_multiplier=0,
                      allow_small_or_imprecise_dtypes=True).then_inc(consts, 1)
            pool.iota(tg[:, :, 0], pattern=[[P, 3]], base=0, channel_multiplier=1,
                      allow_small_or_imprecise_dtypes=True).then_inc(consts, 1)
            pool.wait_ge(consts, 5)
            pool.affine_select(out=ident[:, :], in_=ones[:, :], compare_op=ALU.is_equal, fill=0.0, base=0,
                               pattern=[[-1, P]], channel_multiplier=1).then_inc(consts, 1)
            pool.affine_select(out=tri[:, :], in_=ones[:, :], compare_op=ALU.is_gt, fill=0.0, base=0,
                               pattern=[[1, P]], channel_multiplier=-1).then_inc(consts, 1)
            pool.memset(mask[:, :], 0.0).then_inc(consts, 1)
            pool.wait_ge(consts, 8)
            pool.tensor_copy(identb[:, :], ident[:, :]).then_inc(consts, 1)
            pool.wait_ge(consts, 9)
            pool.memset(mask[0:64, 192:256], NEG).then_inc(consts, 1)
            pool.wait_ge(consts, 10)
            pool.memset(mask[64:128, 0:64], NEG).then_inc(consts, 1)
            pool.wait_ge(consts, 11)
            pool.memset(mask[0:64, 320:384], NEG).then_inc(consts, 1)
            pool.wait_ge(hcat_ready, 16)
            for name, a in (("poolT_prompt", PADP + TP - HIST), ("poolT_sample", PADS + TS - HIST)):
                pool.dma_start(A[name].rearrange("(k p) t -> p k t", p=P), hcat[:, :, a:a + HIST]).then_inc(pool_stored, 16)
        NCONST = 12

        @block.scalar
        def _(act):
            act.dma_start(rows[0:1, :], A["rows"]).then_inc(small_loaded, 16)
            act.dma_start(sinks[:, :], A["sinks"]).then_inc(small_loaded, 16)
            act.dma_start(wr[:, :, :], A["w_router"].rearrange("(k p) n -> p k n", p=P)).then_inc(small_loaded, 16)
            act.dma_start(pT[:, :, :], A["pT"][0].rearrange("(k p) t -> p k t", p=P)).then_inc(p_loaded, 16)
            act.wait_ge(consts, NCONST)
            act.wait_ge(vec_loaded, 16)

            def norm(k):
                for c in range(KC):
                    if k == 0 and c == 0:
                        act.wait_ge(x_loaded, 16)
                    if k > 0:
                        act.wait_ge(x_ready, KC * (k - 1) + c + 1)
                    nc.scalar.activation(sq3[:, c, :], xT[:, c, :], ACT.Square).then_inc(sq_ready, 1)
                act.wait_ge(stat_done, k + 1)
                nc.scalar.activation(std[:, :], PS[:, 7, 0:T], ACT.Sqrt, bias=eps[:, :], scale=1.0 / D).then_inc(std_ready, 1)

            norm(0)
            norm(1)
            act.wait_ge(pool_stored, 32)
            with act.Fori(0, 2) as half:
                for j in range(14):
                    act.wait_ge(g_done, half * 14 + (j + 1))
                    nc.scalar.activation(sg[:, j % 2, :], PS[:, j % 2, 0:T], ACT.Silu).then_inc(silu_done, 1)

            def ple(l):
                for c in range(KC):
                    act.wait_ge(eple_mm, KC * l + c + 1)
                    nc.scalar.activation(ep3[:, c, :], PS[:, c % 2, 0:T], ACT.Copy).then_inc(eple_ready, 1)
                for c in range(KC):
                    act.wait_ge(gate_done, KC * l + c + 1)
                    if c >= 2:
                        act.wait_ge(x_ready, KC * (2 if l == 0 else 5) + c - 1)
                    nc.scalar.activation(sig[:, c % 2, :], PS[:, 2 + c % 2, 0:T], ACT.Sigmoid).then_inc(sig_ready, 1)

            norm(2)
            ple(0)
            norm(3)
            act.dma_start(kTt[:, :, TP:TP + 128], A["cache_kT"].rearrange("(a p) t -> p a t", p=P)).then_inc(cache_loaded, 16)
            act.dma_start(vv[:, 3, :], A["cache_v"]).then_inc(cache_loaded, 16)
            for a in range(2):
                act.wait_ge(k_done, a + 1)
                nc.scalar.activation(kTt[:, a, 0:TP], PS[:, a, 0:TP], ACT.Identity, bias=vec[:, B_K, a:a + 1])
                nc.scalar.activation(kTt[:, a, TP + 128:NKEY], PS[:, a, TP:T], ACT.Identity,
                                     bias=vec[:, B_K, a:a + 1]).then_inc(k_ready, 1)
            for j in range(KC):
                act.wait_ge(q_done, j + 1)
                nc.scalar.activation(qT[:, j, :], PS[:, 4 + j % 2, 0:T], ACT.Identity,
                                     bias=vec[:, B_Q, j:j + 1]).then_inc(q_ready, 1)
            for g in range(4):
                act.wait_ge(max_ready, g + 1)
                if g:
                    act.wait_ge(pT_done, 5 * g)
                neg = st[:, 10:20]
                acc = st[:, 30:40]
                for h in range(4):
                    nc.scalar.activation(pp[:, h, 0:256], PS[:, h, 0:256], ACT.Exp, scale=0.125,
                                         bias=neg[:, h:h + 1], accum_out=acc[:, h:h + 1])
                    nc.scalar.activation(pp[:, h, 256:384], PS[:, h, 256:384], ACT.Exp, scale=0.125,
                                         bias=neg[:, 4 + h:5 + h], accum_out=acc[:, 4 + h:5 + h])
                for jj in range(2):
                    nc.scalar.activation(psm[:, jj, :], PS[:, 4, 192 * jj:192 * jj + 192], ACT.Exp, scale=0.125,
                                         bias=neg[:, 8 + jj:9 + jj], accum_out=acc[:, 8 + jj:9 + jj])
                nc.scalar.activation(st[:, 40:50], st[:, 20:30], ACT.Exp).then_inc(exp_done, 1)
                for n in range(5):
                    act.wait_ge(pT_done, 5 * g + n + 1)
                    if n < 4:
                        nc.scalar.activation(pTh[:, n, :], PS[:, 5 + (5 * g + n) % 2, 0:384], ACT.Copy).then_inc(pT_ready, 1)
                    else:
                        v4 = PS[:, 5 + (5 * g + n) % 2, :].rearrange("p (b n) -> p b n", b=4)
                        nc.scalar.activation(pTs[:, 0:4:2, :], v4[:, 0:4:2, :], ACT.Copy)
                        nc.scalar.activation(pTs[0:64, 1:4:2, :], v4[0:64, 1:4:2, :], ACT.Copy).then_inc(pT_ready, 1)
            norm(4)
            act.wait_ge(top_ready, 1)
            nc.scalar.activation(rt[:, :, 1], rt[:, :, 0], ACT.Exp).then_inc(gexp_ready, 1)
            for n in range(6):
                act.wait_ge(hrow_done, n + 1)
                t, half = n // 2, n % 2
                r = TS if t == 2 else P
                nc.scalar.activation(hrow[0:r, t, 512 * half:512 * half + 512], PS[0:r, 2 + n % 4, :], ACT.Copy).then_inc(hrow_ready, 1)
            def evac_gather(n_before, halfs):
                for hf in halfs:
                    act.wait_ge(gath_done, n_before + (hf + 1))
                    nc.scalar.activation(xg[:, 4 * hf:4 * hf + 4, :], PS[:, 1, :].rearrange("p (k n) -> p k n", k=4),
                                         ACT.Copy).then_inc(xg_ready, 1)

            evac_gather(0, (0, 1))
            act.wait_ge(routed, 1)
            n = act.value_load(extra[0:1, 0:1], min_val=0, max_val=2)
            act.wait_ge(kv_stored, 80)
            with act.Fori(0, n * NE + NE) as i:
                def silu(b):
                    act.wait_ge(unit_done, i * NU + (POS["g", b] + 1))
                    nc.scalar.activation(sgm[:, b % 2, :], PS[:, 2 + 2 * (b % 2), :], ACT.Silu).then_inc(msilu_done, 1)

                def evac_t(b):
                    act.wait_ge(t_done, i * NBK + (b + 1))
                    nc.scalar.activation(guTm[:, 4 * (b % 2):4 * (b % 2) + 4, :],
                                         PS[:, 0, :].rearrange("p (k n) -> p k n", k=4), ACT.Copy).then_inc(t_ready, 1)

                silu(0)
                for b in range(1, NBK):
                    silu(b)
                    evac_t(b - 1)
                evac_gather(i * 2 + 2, (0,))
                evac_t(NBK - 1)
                evac_gather(i * 2 + 2, (1,))
                act.wait_ge(unit_done, i * NU + NU)
                nc.scalar.activation(ysb[:, 0:512], PS[:, 6, :], ACT.Copy).then_inc(y_ready, 1)
            norm(5)
            ple(1)
            norm(6)

        @block.tensor
        def _(pe):
            def mm(out, w, m, start, stop, **kw):
                return nc.tensor.matmul(out, w, m, start=start, stop=stop, **kw)

            pe.wait_ge(consts, NCONST)

            def norm(k):
                for c in range(KC):
                    pe.wait_ge(sq_ready, KC * k + c + 1)
                    last = mm(PS[:, 7, 0:T], ones[:, :], sq3[:, c, :], c == 0, c == KC - 1)
                last.then_inc(stat_done, 1)

            norm(0)
            pe.wait_ge(pool_loaded, 16)
            for c in range(KC):
                g = c // 2
                pe.wait_ge(diff_ready, g + 1)
                if c >= 2:
                    pe.wait_ge(x_ready, c - 1)
                for i in range(2):
                    last = mm(PS[:, c % 2, 0:T], wpool[:, 2 * g + i, P * (c % 2):P * (c % 2) + P], hT[:, 2 * g + i, :], i == 0, i == 1)
                last.then_inc(pool_done, 1)
            norm(1)
            pe.wait_ge(h_ready, 8)
            with pe.Fori(0, 2) as half:
                for z in range(2):
                    pe.wait_ge(quart_loaded[2 * z], half * 16 + 16)
                    pe.wait_ge(quart_loaded[2 * z + 1], half * 16 + 16)
                    w1, w3 = view(ring, 2 * z * QUART, QUART, KC), view(ring, (2 * z + 1) * QUART, QUART, KC)
                    for fl in range(7):
                        j = 7 * z + fl
                        pe.wait_ge(gu_ready, half * 14 + (j + 1))
                        for w, bank, done in ((w1, j % 2, g_done), (w3, 2 + j % 2, u_done)):
                            for k in range(KC):
                                last = mm(PS[:, bank, 0:T], w[:, k, P * fl:P * fl + P], hT[:, k, :], k == 0, k == KC - 1)
                            last.then_inc(done, 1)
            for c in range(KC):
                dp = c // 2
                if c % 2 == 0:
                    pe.wait_ge(quart_loaded[dp], 48)
                w2 = view(ring, dp * QUART, QUART, FC)
                if c >= 2:
                    pe.wait_ge(x_ready, KC + c - 1)
                for f in range(FC):
                    if c == 0:
                        pe.wait_ge(gu_ready, f + 3)
                    last = mm(PS[:, 4 + c % 2, 0:T], w2[:, f, P * (c % 2):P * (c % 2) + P], guT[:, f, :], f == 0, f == FC - 1)
                last.then_inc(down_done, 1)

            def ple(l):
                pe.wait_ge(proj_loaded, 16 * (l + 1))
                pe.wait_ge(p_loaded, 16 * (l + 1))
                for c in range(KC):
                    if c >= 2:
                        pe.wait_ge(eple_ready, KC * l + c - 1)
                    for k in range(2):
                        last = mm(PS[:, c % 2, 0:T], proj[:, k, P * c:P * c + P], pT[:, k, :], k == 0, k == 1)
                    last.then_inc(eple_mm, 1)
                pe.wait_ge(gate_loaded, 16 * (l + 1))
                pe.wait_ge(h_ready, 16 if l == 0 else 48)
                for c in range(KC):
                    if c >= 2:
                        pe.wait_ge(sig_ready, KC * l + c - 1)
                    for k in range(KC):
                        last = mm(PS[:, 2 + c % 2, 0:T], wgate[:, k, P * c:P * c + P], hT[:, k, :], k == 0, k == KC - 1)
                    last.then_inc(gate_done, 1)

            norm(2)
            ple(0)
            norm(3)
            pe.wait_ge(kv_loaded, 32)
            pe.wait_ge(small_loaded, 48)
            pe.wait_ge(h_ready, 24)
            for a in range(2):
                for k in range(KC):
                    last = mm(PS[:, a, 0:T], wk[:, k, P * a:P * a + P], kvT[:, k, :], k == 0, k == KC - 1)
                last.then_inc(k_done, 1)
            for t in range(3):
                r = TS if t == 2 else P
                if t == 2:
                    pe.wait_ge(v_ready, 1)
                out = PS[0:r, 2 + t % 2, 0:256]
                for k in range(KC):
                    mm(out, kvT[:, k, P * t:P * t + r], wv[:, k, :], k == 0, False)
                mm(out, ones[0:1, 0:r], rows[0:1, 0:256], False, True).then_inc(v_done, 1)
            pe.wait_ge(wq_loaded, 16)
            pe.wait_ge(h_ready, 32)
            for j in range(KC):
                if j >= 2:
                    pe.wait_ge(q_ready, j - 1)
                for k in range(KC):
                    last = mm(PS[:, 4 + j % 2, 0:T], wq[:, k, P * j:P * j + P], hT[:, k, :], k == 0, k == KC - 1)
                last.then_inc(q_done, 1)
            pe.wait_ge(k_ready, 2)
            pe.wait_ge(v_ready, 4)
            pe.wait_ge(cache_loaded, 32)

            def scores(g):
                for jj in range(2):
                    j = 2 * g + jj
                    a = j // 4
                    pe.wait_ge(q_ready, KC)
                    for b in range(2):
                        bank, o = 2 * jj + b, 64 * b
                        mm(PS[:, bank, 0:384], identb[:, :], mask[:, :], True, False, skip_group_check=True)
                        mm(PS[:, bank, 0:256], qT[o:o + 64, j, P:2 * P], kTt[o:o + 64, a, 0:TP], False, False, skip_group_check=True)
                        mm(PS[:, bank, 256:384], qT[o:o + 64, j, 0:P], kTt[o:o + 64, a, 0:P], False, True, skip_group_check=True)
                    for b in range(2):
                        o = 64 * b
                        last = mm(PS[o:o + 64, 4, 192 * jj:192 * jj + 192], qT[o:o + 64, j, TP:T], kTt[o:o + 64, a, TP:NKEY], True, True)
                last.then_inc(score_done, 1)

            scores(0)
            for g in range(4):
                for n in range(5):
                    m = 5 * g + n
                    pe.wait_ge(p_ready, m + 1)
                    if m >= 2:
                        pe.wait_ge(pT_ready, m - 1)
                    bank = 5 + m % 2
                    for blk in range(3 if n < 4 else 4):
                        if n < 4:
                            src, out = pp[:, n, P * blk:P * blk + P], PS[:, bank, P * blk:P * blk + P]
                        else:
                            w = P if blk % 2 == 0 else 64
                            src, out = psm[:, blk // 2, P * (blk % 2):P * (blk % 2) + w], PS[0:w, bank, P * blk:P * blk + P]
                        last = nc.tensor.transpose(out, src, ident[:, :])
                    last.then_inc(pT_done, 1)
                if g < 3:
                    pe.wait_ge(exp_done, g + 1)
                    scores(g + 1)
                pe.wait_ge(pT_ready, 5 * g + 5)
                for jj in range(2):
                    j = 2 * g + jj
                    a = j // 4
                    if j:
                        pe.wait_ge(o_ready, j)
                    for b in range(2):
                        o, h = 64 * b, 2 * jj + b
                        vc = 64 * (2 * a + b)
                        mm(PS[o:o + 64, 7, P:2 * P], vv[:, 0, vc:vc + 64], pTh[:, h, 0:P], True, False)
                        mm(PS[o:o + 64, 7, P:2 * P], vv[:, 1, vc:vc + 64], pTh[:, h, P:2 * P], False, True)
                        mm(PS[o:o + 64, 7, 0:P], vv[:, 0, vc:vc + 64], pTh[:, h, 2 * P:3 * P], True, True)
                        mm(PS[o:o + 64, 7, TP:T], vv[:, 3, vc:vc + 64], pTs[:, 2 * jj, o:o + 64], True, False)
                        last = mm(PS[o:o + 64, 7, TP:T], vv[0:64, 2, vc:vc + 64], pTs[0:64, 2 * jj + 1, o:o + 64], False, True)
                    last.then_inc(pv_done, 1)
            pe.wait_ge(wo_loaded, 16)
            pe.wait_ge(o_ready, 8)
            for c in range(KC):
                if c >= 2:
                    pe.wait_ge(x_ready, 3 * KC + c - 1)
                for j in range(KC):
                    last = mm(PS[:, c % 2, 0:T], wo[:, j, P * c:P * c + P], oT[:, j, :], j == 0, j == KC - 1)
                last.then_inc(oproj_done, 1)
            norm(4)
            pe.wait_ge(h_ready, 40)
            for t in range(3):
                r = TS if t == 2 else P
                out = PS[0:r, 0, 8 * t:8 * t + 8]
                for k in range(KC):
                    mm(out, hT[:, k, P * t:P * t + r], wr[:, k, :], k == 0, False)
                last = mm(out, ones[0:1, 0:r], rows[0:1, 256:256 + NE], False, True)
            last.then_inc(lg_done, 1)
            for n in range(6):
                t, half = n // 2, n % 2
                r = TS if t == 2 else P
                if n >= 4:
                    pe.wait_ge(hrow_ready, n - 3)
                for q in range(4):
                    last = nc.tensor.transpose(PS[0:r, 2 + n % 4, P * q:P * q + P], hT[:, 4 * half + q, P * t:P * t + r], ident[:, :])
                last.then_inc(hrow_done, 1)
            pe.wait_ge(sel_ready, 1)
            for t in range(4):
                for s in range(min(t, 2) + 1):
                    w = tri if s == t else ones
                    last = mm(PS[:, 1, 8 * t:8 * t + 8], w[:, :], sel[:, s, :], s == 0, s == min(t, 2))
            last.then_inc(pos_done, 1)
            pe.wait_ge(hrow_ready, 6)

            def gather(i, hf, nth):
                for c in range(4 * hf, 4 * hf + 4):
                    for t in range(3):
                        r = TS if t == 2 else P
                        last = mm(PS[:, 1, P * (c % 4):P * (c % 4) + P], hrow[0:r, t, P * c:P * c + P], Pm[0:r, t, :], t == 0, t == 2)
                last.then_inc(gath_done, 1)

            def slot_info():
                for t in range(3):
                    last = mm(PS[:, 1, 0:2], Pm[:, t, :], tg[:, t, :], t == 0, t == 2)
                last.then_inc(slots_done, 1)

            pe.wait_ge(P_ready, 1)
            gather(0, 0, 0)
            pe.wait_ge(xg_ready, 1)
            gather(0, 1, 0)
            pe.wait_ge(xg_ready, 2)
            slot_info()

            def scatter(c):
                mm(PS[:, 1, 0:T], ysb[:, P * c:P * c + P], PT, True, True).then_inc(scat_done, 1)

            pe.wait_ge(routed, 1)
            n = pe.value_load(extra[0:1, 0:1], min_val=0, max_val=2)
            with pe.Fori(0, n * NE + NE) as i:
                def arrived(u):
                    pe.wait_ge(slot_loaded[u % NSLOT], i * 48 + 16 * (u // NSLOT + 1))

                pend = list(range(KC))

                def scatter_next():
                    c = pend.pop(0)
                    if c == 0:
                        pe.wait_ge(y_ready, i * 2 + 2)
                        pe.wait_ge(PT_ready, i + 1)
                        pe.wait_ge(si_ready, i + 1)
                    else:
                        pe.wait_ge(y_added, i * KC + c)
                    scatter(c)

                def up(kind, b):
                    u = POS[kind, b]
                    w = slot(u).rearrange("p (k n) -> p k n", k=KC)
                    bank = 2 + 2 * (b % 2) + (kind == "u")
                    arrived(u)
                    if kind == "g" and b == 0:
                        pe.wait_ge(xg_ready, i * 2 + 2)
                    if kind == "g" and b != 1:
                        pe.wait_ge(gum_ready, i * NBK + (b + 1 if b == 0 else b))
                    for k in range(KC):
                        last = mm(PS[:, bank, :], xg[:, k, :], w[:, k, :], k == 0, k == KC - 1)
                        if k % 3 == 2 and pend:
                            scatter_next()
                    last.then_inc(unit_done, 1)

                def transposes(b):
                    pe.wait_ge(gum_ready, i * NBK + (b + 2))
                    pe.wait_ge(t_ready, i * NBK + (b + 1))
                    for q in range(4):
                        last = nc.tensor.transpose(PS[:, 0, P * q:P * q + P], gum[:, b % 2, P * q:P * q + P], ident[:, :])
                    last.then_inc(t_done, 1)

                def down(b):
                    u = POS["d", b]
                    w = slot(u).rearrange("p (f n) -> p f n", f=4)
                    arrived(u)
                    pe.wait_ge(t_ready, i * NBK + (b + 2))
                    for f in range(4):
                        for hf in range(2):
                            last = mm(PS[:, 6 + hf, :], guTm[:, 4 * (b % 2) + f, :], w[:, f, 512 * hf:512 * hf + 512],
                                      b == 0 and f == 0, b == NBK - 1 and f == 3)
                    last.then_inc(unit_done, 1)

                up("g", 0)
                up("u", 0)
                for b in range(1, NBK):
                    up("g", b)
                    while pend:
                        scatter_next()
                    transposes(b - 1)
                    up("u", b)
                    down(b - 1)
                pe.wait_ge(P_ready, i + 2)
                pe.wait_ge(y_added, i * KC + KC)
                gather(i, 0, 1)
                transposes(NBK - 1)
                pe.wait_ge(xg_ready, i * 2 + 3)
                gather(i, 1, 1)
                down(NBK - 1)
                pe.wait_ge(xg_ready, i * 2 + 4)
                slot_info()
            pe.wait_ge(y_ready, n * (2 * NE) + (2 * NE + 2))
            pe.wait_ge(PT_ready, n * NE + (NE + 1))
            pe.wait_ge(si_ready, n * NE + (NE + 1))
            for c in range(KC):
                if c:
                    pe.wait_ge(y_added, n * (NE * KC) + (NE * KC + c))
                scatter(c)
            norm(5)
            ple(1)
            norm(6)

        @block.vector
        def _(v):
            links = [0]

            def link(ins):
                links[0] += 1
                ins.then_inc(chain, 1)
                v.wait_ge(chain, links[0])

            def norm(k):
                v.wait_ge(std_ready, k + 1)
                link(nc.vector.reciprocal(rstd[:, :], std[:, :]))

            def scaled(g, dest, done):
                for c in range(KC):
                    nc.vector.scalar_tensor_tensor(out=dest[:, c, :], in0=xT[:, c, :], scalar=vec[:, g, c:c + 1], in1=rstd[:, :],
                                                   op0=ALU.mult, op1=ALU.mult).then_inc(done, 1)

            v.sem_inc(gu_ready, 2)
            v.sem_inc(t_ready, 1)
            v.sem_inc(gum_ready, 1)
            v.sem_inc(PT_ready, 1)
            v.sem_inc(y_ready, 2)
            v.wait_ge(consts, NCONST)
            link(nc.vector.tensor_copy(st[:, 0:16], iota_i[:, :]))
            link(nc.vector.reciprocal(st[:, 16:32], st[:, 0:16]))
            for g, w in enumerate((2, 4, 8, 16)):
                nc.vector.memset(invc[:, g, w - 1:T], 1.0 / w)
                last = nc.vector.tensor_copy(invc[:, g, 0:w - 1], st[:, 16:16 + w - 1])
            link(last)
            norm(0)
            for c in range(KC):
                for a, b, o in ((0, TP, PADP), (TP, T, PADS)):
                    nc.vector.scalar_tensor_tensor(out=hcat[:, c, o:o + b - a], in0=xT[:, c, a:b], scalar=vec[:, G_MIX0, c:c + 1],
                                                   in1=rstd[:, a:b], op0=ALU.mult, op1=ALU.mult).then_inc(hcat_ready, 1)
            v.wait_ge(hcat_ready, 16)
            v.wait_ge(hzero, 1)
            v.wait_ge(hist_loaded, 16)
            link(nc.vector.tensor_tensor(sA[:, :, 1:], hcat[:, :, 1:], hcat[:, :, 0:LCAT - 1], ALU.add))

            def diff(g, s):
                for o, a, n in ((PADP, 0, TP), (PADS, TP, TS)):
                    nc.vector.tensor_tensor(hT[:, 2 * g:2 * g + 2, a:a + n], s[:, 2 * g:2 * g + 2, o:o + n],
                                            invc[:, g:g + 1, a:a + n].broadcast_to([P, 2, n]), ALU.mult).then_inc(chain, 1)
                    links[0] += 1
                v.wait_ge(chain, links[0])
                for o, a, n in ((PADP, 0, TP), (PADS, TP, TS)):
                    last = nc.vector.tensor_tensor(hT[:, 2 * g:2 * g + 2, a:a + n], hT[:, 2 * g:2 * g + 2, a:a + n],
                                                   hcat[:, 2 * g:2 * g + 2, o:o + n], ALU.subtract)
                last.then_inc(diff_ready, 1)

            diff(0, sA)
            link(nc.vector.tensor_tensor(sB[:, 2:, 3:], sA[:, 2:, 3:], sA[:, 2:, 1:LCAT - 2], ALU.add))
            diff(1, sB)
            link(nc.vector.tensor_tensor(sA[:, 4:, 7:], sB[:, 4:, 7:], sB[:, 4:, 3:LCAT - 4], ALU.add))
            diff(2, sA)
            link(nc.vector.tensor_tensor(sB[:, 6:, 15:], sA[:, 6:, 15:], sA[:, 6:, 7:LCAT - 8], ALU.add))
            diff(3, sB)
            for c in range(KC):
                v.wait_ge(pool_done, c + 1)
                nc.vector.scalar_tensor_tensor(out=xT[:, c, :], in0=PS[:, c % 2, 0:T], scalar=vec[:, POOL_SC, c:c + 1],
                                               in1=xT[:, c, :], op0=ALU.mult, op1=ALU.add).then_inc(x_ready, 1)
            norm(1)
            scaled(G_FFN0, hT, h_ready)
            v.wait_ge(pool_stored, 32)
            with v.Fori(0, 2) as half:
                for j in range(14):
                    v.wait_ge(silu_done, half * 14 + (j + 1))
                    v.wait_ge(u_done, half * 14 + (j + 1))
                    nc.vector.tensor_tensor(G[:, bass.ds((half * 14 + j) * T, T)], sg[:, j % 2, :], PS[:, 2 + j % 2, 0:T],
                                            ALU.mult).then_inc(gu_ready, 1)

            def add_product(done, base, bank):
                for c in range(KC):
                    v.wait_ge(done, base + c + 1)
                    nc.vector.tensor_tensor(xT[:, c, :], xT[:, c, :], PS[:, bank + c % 2, 0:T], ALU.add).then_inc(x_ready, 1)

            def ple(l):
                v.wait_ge(eple_ready, KC * l + KC)
                for c in range(KC):
                    v.wait_ge(sig_ready, KC * l + c + 1)
                    link(nc.vector.tensor_tensor(gtm[:, c % 2, :], sig[:, c % 2, :], ep3[:, c, :], ALU.mult))
                    nc.vector.tensor_tensor(xT[:, c, :], xT[:, c, :], gtm[:, c % 2, :], ALU.add).then_inc(x_ready, 1)

            add_product(down_done, 0, 4)
            norm(2)
            scaled(G_PLE0, hT, h_ready)
            ple(0)
            norm(3)
            scaled(G_KV, kvT, h_ready)
            scaled(G_MIX1, hT, h_ready)
            for t in range(3):
                r = TS if t == 2 else P
                v.wait_ge(v_done, t + 1)
                nc.vector.tensor_copy(vv[0:r, t, :], PS[0:r, 2 + t % 2, 0:256]).then_inc(v_ready, 1)
            v.sem_inc(v_ready, 1)
            for g in range(4):
                v.wait_ge(score_done, g + 1)
                if g == 0:
                    v.wait_ge(small_loaded, 48)
                mx, neg, ds_, acc, es = (st[:, 10 * i:10 * i + 10] for i in range(5))
                nc.vector.reduce_max(mx[:, 0:4], PS[:, 0:4, 0:256], AX.X)
                nc.vector.reduce_max(mx[:, 4:8], PS[:, 0:4, 256:384], AX.X)
                link(nc.vector.reduce_max(mx[:, 8:10], PS[:, 4, 0:384].rearrange("p (j n) -> p j n", j=2), AX.X))
                link(nc.vector.scalar_tensor_tensor(out=mx, in0=mx, scalar=0.125, in1=sinks[:, 10 * g:10 * g + 10], op0=ALU.mult, op1=ALU.max))
                nc.vector.tensor_scalar(neg, mx, -1.0, None, ALU.mult)
                nc.vector.tensor_tensor(ds_, sinks[:, 10 * g:10 * g + 10], mx, ALU.subtract).then_inc(max_ready, 1)
                v.wait_ge(exp_done, g + 1)
                link(nc.vector.tensor_tensor(acc, acc, es, ALU.add))
                link(nc.vector.reciprocal(acc, acc))
                for h in range(4):
                    nc.vector.tensor_scalar(pp[:, h, 0:256], pp[:, h, 0:256], acc[:, h:h + 1], None, ALU.mult)
                    nc.vector.tensor_scalar(pp[:, h, 256:384], pp[:, h, 256:384], acc[:, 4 + h:5 + h], None, ALU.mult).then_inc(p_ready, 1)
                for jj in range(2):
                    last = nc.vector.tensor_scalar(psm[:, jj, :], psm[:, jj, :], acc[:, 8 + jj:9 + jj], None, ALU.mult)
                last.then_inc(p_ready, 1)
                for jj in range(2):
                    v.wait_ge(pv_done, 2 * g + jj + 1)
                    nc.vector.tensor_copy(oT[:, 2 * g + jj, :], PS[:, 7, 0:T]).then_inc(o_ready, 1)
            add_product(oproj_done, 0, 0)
            norm(4)
            scaled(G_FFN1, hT, h_ready)
            for z in (lg, gate, sel):
                nc.vector.memset(z[:, :, :], 0.0).then_inc(chain, 1)
                links[0] += 1
            v.wait_ge(kv_stored, 80)
            nc.vector.memset(ysb, 0.0).then_inc(chain, 1)
            nc.vector.memset(PT, 0.0).then_inc(chain, 1)
            links[0] += 2
            v.wait_ge(chain, links[0])
            v.wait_ge(lg_done, 1)
            nc.vector.tensor_copy(lg[:, 0:2, :], PS[:, 0, 0:16].rearrange("p (t e) -> p t e", t=2))
            link(nc.vector.tensor_copy(lg[0:TS, 2, :], PS[0:TS, 0, 16:24]))
            for t in range(3):
                link(nc.vector.max(top[:, t, :], lg[:, t, :]))
                link(nc.vector.max_index(topi[:, t, :], top[:, t, :], lg[:, t, :]))
            nc.vector.tensor_tensor(rt[:, :, 0], top[:, :, 1], top[:, :, 0], ALU.subtract).then_inc(top_ready, 1)
            link(nc.vector.tensor_copy(rt[:, :, 2:4], topi[:, :, 0:2]))
            v.wait_ge(gexp_ready, 1)
            link(nc.vector.tensor_scalar(rt[:, :, 0], rt[:, :, 1], 1.0, None, ALU.add))
            link(nc.vector.reciprocal(rt[:, :, 0], rt[:, :, 0]))
            link(nc.vector.tensor_tensor(rt[:, :, 1], rt[:, :, 1], rt[:, :, 0], ALU.mult))
            for t in range(3):
                r = TS if t == 2 else P
                nc.vector.tensor_scalar(sel[0:r, t, :], iota[0:r, 0:NE], rt[0:r, t, 2:3], None, ALU.is_equal)
                link(nc.vector.tensor_scalar(oh[0:r, t, :], iota[0:r, 0:NE], rt[0:r, t, 3:4], None, ALU.is_equal))
                link(nc.vector.tensor_scalar(gate[0:r, t, :], sel[0:r, t, :], rt[0:r, t, 0:1], None, ALU.mult))
                link(nc.vector.scalar_tensor_tensor(out=gate[0:r, t, :], in0=oh[0:r, t, :], scalar=rt[0:r, t, 1:2], in1=gate[0:r, t, :],
                                                    op0=ALU.mult, op1=ALU.add))
                link(nc.vector.tensor_tensor(sel[0:r, t, :], sel[0:r, t, :], oh[0:r, t, :], ALU.add))
            v.sem_inc(sel_ready, 1)
            v.wait_ge(pos_done, 1)
            link(nc.vector.scalar_tensor_tensor(out=posm[:, :, :], in0=PS[:, 1, 0:24].rearrange("p (t e) -> p t e", t=3), scalar=1.0,
                                                in1=sel[:, :, :], op0=ALU.add, op1=ALU.mult))
            nc.vector.tensor_scalar(posm[:, :, :], posm[:, :, :], -1.0, None, ALU.add).then_inc(stepped, 1)
            link(nc.vector.reduce_max(cnt[0:1, 0:1], PS[0:1, 1, 24:32], AX.X))
            nc.vector.tensor_scalar(cnt[0:1, 1:2], cnt[0:1, 0:1], float(P), None, ALU.is_gt)
            link(nc.vector.tensor_scalar(cnt[0:1, 2:3], cnt[0:1, 0:1], float(2 * P), None, ALU.is_gt))
            link(nc.vector.tensor_tensor(cnt[0:1, 3:4], cnt[0:1, 1:2], cnt[0:1, 2:3], ALU.add))
            nc.vector.tensor_copy(extra[0:1, 0:1], cnt[0:1, 3:4]).then_inc(routed, 1)

            def one_hots(e, steps):
                v.wait_ge(stepped, steps)
                for t in range(3):
                    nc.vector.tensor_scalar(Pm[:, t, :], iota[:, 0:P], posm[:, t, bass.ds(e, 1)], None, ALU.is_equal)
                nc.vector.tensor_copy(tg[:, :, 1:2], gate[:, :, bass.ds(e, 1)]).then_inc(P_ready, 1)
                v.wait_ge(P_ready, steps)
                nc.vector.tensor_scalar(posm[:, :, bass.ds(e, 1)], posm[:, :, bass.ds(e, 1)], float(-P), None, ALU.add).then_inc(stepped, 1)

            def take_slots(count):
                v.wait_ge(slots_done, count)
                nc.vector.tensor_copy(si[:, :], PS[:, 1, 0:2]).then_inc(si_ready, 1)

            one_hots(0, 1)
            take_slots(1)
            v.wait_ge(routed, 1)
            n = v.value_load(extra[0:1, 0:1], min_val=0, max_val=2)

            def add_back(c, count):
                v.wait_ge(scat_done, count)
                nc.vector.tensor_tensor(xT[:, c, :], xT[:, c, :], PS[:, 1, 0:T], ALU.add).then_inc(y_added, 1)

            v.wait_ge(kv_stored, 80)
            with v.Fori(0, n * NE + NE) as i:
                def glu(b):
                    v.wait_ge(msilu_done, i * NBK + (b + 1))
                    v.wait_ge(unit_done, i * NU + (POS["u", b] + 1))
                    nc.vector.tensor_tensor(gum[:, b % 2, :], sgm[:, b % 2, :], PS[:, 3 + 2 * (b % 2), :], ALU.mult).then_inc(gum_ready, 1)

                for c in range(4):
                    add_back(c, i * KC + (c + 1))
                glu(0)
                for c in range(4, KC):
                    add_back(c, i * KC + (c + 1))
                v.wait_ge(si_ready, i + 1)
                nc.vector.tensor_scalar(PT, iota[:, :], si[:, 0:1], si[:, 1:2], ALU.is_equal, ALU.mult).then_inc(PT_ready, 1)
                glu(1)
                glu(2)
                one_hots((i + 1) % NE, i + 2)
                for b in range(3, NBK):
                    glu(b)
                v.wait_ge(unit_done, i * NU + NU)
                nc.vector.tensor_copy(ysb[:, 512:1024], PS[:, 7, :]).then_inc(y_ready, 1)
                take_slots(i + 2)
            for c in range(KC):
                add_back(c, n * (NE * KC) + (NE * KC + c + 1))
            v.wait_ge(y_added, n * (NE * KC) + (NE * KC + KC))
            v.sem_inc(x_ready, KC)
            norm(5)
            scaled(G_PLE1, hT, h_ready)
            ple(1)
            norm(6)
            scaled(G_FIN, hT, h_ready)


def kernel(**inputs):
    import numpy as np
    import concourse.bacc as bacc
    from concourse.bass_utils import run_bass_kernel_spmd as run

    a = {k: np.asarray(x) for k, x in inputs.items()}

    def chunks(x):
        return x.reshape(KC, P).T

    heads = [(2 * aa + b) * 4 + r for aa in range(2) for r in range(4) for b in range(2)]
    bq = a["b_q"][0].reshape(16, 64)[heads].reshape(KC, P).T
    bk = np.zeros((P, KC), a["b_k"].dtype)
    bk[:, 0:2] = a["b_k"].reshape(2, P).T
    vecs = [chunks(a["g_mix"][0]), chunks(a["g_ffn"][0]), chunks(a["g_ple"][0]), chunks(a["g_kv"]), chunks(a["g_mix"][1]),
            chunks(a["g_ffn"][1]), chunks(a["g_ple"][1]), chunks(a["g_final"]), chunks(a["pool_scale"][0]), bq, bk]
    sk = a["sinks"][0]
    sink = np.zeros((P, 40), sk.dtype)
    for g in range(4):
        for n in range(4):
            h = heads[4 * g + n]
            sink[:, 10 * g + n] = sk[h]
            sink[:, 10 * g + 4 + n] = sk[h]
            sink[64 * (n % 2):64 * (n % 2) + 64, 10 * g + 8 + n // 2] = sk[h]
    ins = {
        "xT": np.concatenate([a["x_prompt"][0], a["x_sample"][0]], 0).T,
        "pT": np.concatenate([a["p_prompt"][:, 0], a["p_sample"][:, 0]], 1).transpose(0, 2, 1),
        "histT": a["state_pool"][0, 0].T,
        "vec": np.stack(vecs, 1),
        "rows": np.concatenate([a["b_v"], a["b_router"][0]])[None],
        "sinks": sink,
        "cache_kT": a["cache_k"][0].transpose(1, 2, 0).reshape(256, 128),
        "cache_v": a["cache_v"][0].reshape(128, 256),
        "w_pool": a["w_pool"][0], "w_k": a["w_k"], "w_v": a["w_v"],
        "w_q": a["w_q"][0].reshape(D, 16, 64)[:, heads].reshape(D, D),
        "w_o": a["w_o"][0].reshape(16, 64, D)[heads].reshape(D, D),
        "w1_dense": a["w1_dense"][0], "w3_dense": a["w3_dense"][0], "w2_dense": a["w2_dense"][0],
        "w_router": a["w_router"][0], "w1_moe": a["w1_moe"][0], "w3_moe": a["w3_moe"][0], "w2_moe": a["w2_moe"][0],
        "w_ple_proj": a["w_ple_proj"], "w_ple_gate": a["w_ple_gate"],
    }
    outs = {"yT": (D, T), "poolT_prompt": (D, HIST), "poolT_sample": (D, HIST), "kT_prompt": (256, 128), "kT_sample": (256, 128),
            "v_prompt": (128, 256), "v_sample": (128, 256)}
    nc = bacc.Bacc("TRN2", target_bir_lowering=False, num_devices=1)
    A, arrays = {}, {}
    for name, x in ins.items():
        arrays["in_" + name] = np.ascontiguousarray(x)
        A[name] = nc.dram_tensor("in_" + name, x.shape, mybir.dt.from_np(x.dtype), kind="ExternalInput").ap()
    for name, shape in outs.items():
        A[name] = nc.dram_tensor("out_" + name, shape, F32, kind="ExternalOutput").ap()
    build(nc, A)
    r = run(nc, [arrays], core_ids=[0]).results[0]
    o = {name: np.asarray(r["out_" + name]) for name in outs}
    y = o["yT"].T

    def keys(x):
        return np.ascontiguousarray(x.reshape(4, 64, 128).transpose(2, 0, 1))[None]

    return (np.ascontiguousarray(y[:TP])[None], np.ascontiguousarray(y[TP:])[None],
            np.ascontiguousarray(o["poolT_prompt"].T)[None, None], np.ascontiguousarray(o["poolT_sample"].T)[None, None],
            keys(o["kT_prompt"]), o["v_prompt"].reshape(1, 128, 4, 64), keys(o["kT_sample"]), o["v_sample"].reshape(1, 128, 4, 64))
```

```python
import concourse.bass as bass
from concourse import mybir
from contextlib import ExitStack

F32 = mybir.dt.float32
F32R = mybir.dt.float32r
BF16 = mybir.dt.bfloat16
I32 = mybir.dt.int32
U32 = mybir.dt.uint32
ALU = mybir.AluOpType
ACT = mybir.ActivationFunctionType
AX = mybir.AxisListType

P = 128
D, TP, TS = 1024, 256, 64
T = TP + TS
KC = D // P
FF = 3584
FC = FF // P
NE = 8
HIST = 15
PADP, PADS = HIST, HIST + TP + HIST
LCAT = PADS + TS
PLE = 256
NEG = -1e30
EPS = 1e-6
G_MIX0, G_FFN0, G_PLE0, G_KV, G_MIX1, G_FFN1, G_PLE1, G_FIN, POOL_SC, B_Q, B_K, B_V = range(12)
NVEC = 12

UNIT, NRAW, NSPL = 2048, 6, 3
Q_POOL = 0
Q_UP = 1
NUP = FF // 256
Q_DOWN = Q_UP + 2 * NUP
Q_PROJ = Q_DOWN + NUP
Q_GATE = Q_PROJ + 1
Q_K, Q_V = Q_GATE + 4, Q_GATE + 5
Q_Q = Q_V + 1
Q_O = Q_Q + 4
Q_MOE = Q_O + 4
NBK = 7
SEQ = [("g", 0), ("u", 0)]
for _b in range(1, NBK):
    SEQ += [("g", _b), ("u", _b), ("d", _b - 1)]
SEQ += [("d", NBK - 1)]
NU = 2 * len(SEQ)
POS = {s: 2 * n for n, s in enumerate(SEQ)}
QBANK = (0, 2, 6, 4)
PVBANK = (7, 4)
assert NU % NRAW == 0 and NU % NSPL == 0 and NRAW % NSPL == 0
RND = NU // NRAW


def build(nc, A):
    ctx = ExitStack()
    with ctx:
        def sb(name, shape, dt=F32):
            return ctx.enter_context(nc.sbuf_tensor("s_" + name, shape, dt))

        def sem(name):
            return ctx.enter_context(nc.semaphore(name))

        PS = ctx.enter_context(nc.psum_tensor("PS", [P, 8, 512], F32))
        raw = sb("raw", [P, NRAW, UNIT])
        Sh, Sl = sb("Sh", [P, NSPL, UNIT], F32R), sb("Sl", [P, NSPL, UNIT], F32R)
        NA = KC * T + 2 * T
        Ah, Al = sb("Ah", [P, NA], F32R), sb("Al", [P, NA], F32R)
        G = sb("G", [P, FC * T])
        xT = sb("xT", [P, KC, T])
        hT = sb("hT", [P, KC, T])
        sq = sb("sq", [P, KC * T])
        pT = sb("pT", [P, 2 * T])
        vec = sb("vec", [P, NVEC, KC])
        std = sb("std", [P, T])
        rstd = sb("rstd", [P, T])
        eps = sb("eps", [P, 1])
        ones = sb("ones", [P, P])
        ident = sb("ident", [P, P])
        tri = sb("tri", [P, P])
        identb = sb("identb", [P, P], BF16)
        mask = sb("mask", [P, 384], BF16)
        iota_i = sb("iota_i", [P, 16], I32)
        inv = sb("inv", [P, 16])
        iota = sb("iota", [P, T])
        wr = sb("wr", [P, KC, NE])
        rows = sb("rows", [1, NE])
        sinks = sb("sinks", [P, 40])
        st = sb("st", [P, 50])
        lg = sb("lg", [P, 3, NE])
        top = sb("top", [P, 3, NE])
        topi = sb("topi", [P, 3, NE], U32)
        rt = sb("rt", [P, 3, 4])
        oh = sb("oh", [P, 3, NE])
        gate = sb("gate", [P, 3, NE])
        sel = sb("sel", [P, 3, NE])
        posm = sb("posm", [P, 3, NE])
        tg = sb("tg", [P, 3, 2])
        si = sb("si", [P, 2])
        cnt = sb("cnt", [1, 4])
        extra = sb("extra", [1, 1], I32)
        PT = sb("PT", [P, T], F32R)

        def view(t, a, n, k=None):
            v = t[:, a:a + n]
            return v if k is None else v.rearrange("p (k n) -> p k n", k=k)

        sq3 = view(sq, 0, KC * T, KC)
        Ah3, Al3 = view(Ah, 0, KC * T, KC), view(Al, 0, KC * T, KC)
        pAh, pAl = view(Ah, KC * T, 2 * T, 2), view(Al, KC * T, 2 * T, 2)
        L8 = KC * LCAT
        hcat, sA, sB = view(G, 0, L8, KC), view(G, L8, L8, KC), view(G, 2 * L8, L8, KC)
        sg = view(sq, 0, 2 * T, 2)
        guT = view(G, 0, FC * T, FC)
        GUOFF = (KC * T, 0, 2 * T)
        sig, gtm, ep3 = view(G, 0, 2 * T, 2), view(G, 2 * T, 2 * T, 2), view(G, 4 * T, KC * T, KC)
        NKEY = TP + 128 + TS
        qT = view(G, 0, KC * T, KC)
        kTt = view(G, KC * T, 2 * NKEY, 2)
        vv = view(G, KC * T + 2 * NKEY, 1024, 4)
        pb0 = KC * T + 2 * NKEY + 1024
        pp = view(G, pb0, 4 * 384, 4)
        psm = view(G, pb0 + 4 * 384, 512, 2)
        vT = view(sq, 0, 2 * T, 2)
        pTr = view(sq, 0, 2048, 4)
        m0 = pb0
        hrow = view(G, m0, 3 * D, 3)
        sgm, gum = view(G, 0, 1024, 2), view(G, 1024, 1024, 2)
        Pm = view(G, 2048, 384, 3)
        xgh, xgl = view(Ah, 0, KC * P, KC), view(Al, 0, KC * P, KC)
        gth, gtl = view(Ah, 1024, 1024, 8), view(Al, 1024, 1024, 8)
        ysh, ysl = view(Ah, 2048, 1024), view(Al, 2048, 1024)

        x_loaded, vec_loaded, small_loaded, hist_loaded, p_loaded, cache_loaded = (sem(n) for n in (
            "x_loaded", "vec_loaded", "small_loaded", "hist_loaded", "p_loaded", "cache_loaded"))
        raw_loaded = [sem(f"raw_loaded{s}") for s in range(NRAW)]
        pool_stored, kv_stored, y_stored = sem("pool_stored"), sem("kv_stored"), sem("y_stored")
        hi_ready, lo_ready, unit_done = sem("hi_ready"), sem("lo_ready"), sem("unit_done")
        slots_freed = sem("slots_freed")
        consts, hzero, chain = sem("consts"), sem("hzero"), sem("chain")
        sq_ready, stat_done, std_ready, x_ready = sem("sq_ready"), sem("stat_done"), sem("std_ready"), sem("x_ready")
        h_ready, hh_ready, hl_ready, hcat_ready = sem("h_ready"), sem("hh_ready"), sem("hl_ready"), sem("hcat_ready")
        ph_ready, pl_ready = sem("ph_ready"), sem("pl_ready")
        silu_done, gu_ready, gh_ready, gl_ready = sem("silu_done"), sem("gu_ready"), sem("gh_ready"), sem("gl_ready")
        eple_ready, sig_ready = sem("eple_ready"), sem("sig_ready")
        k_ready, vT_ready, vt_done, v_ready, q_ready = (sem(n) for n in ("k_ready", "vT_ready", "vt_done", "v_ready", "q_ready"))
        score_done, max_ready, exp_done, p_ready = sem("score_done"), sem("max_ready"), sem("exp_done"), sem("p_ready")
        pT_done, pT_ready, pv_done, oh_ready, ol_ready = sem("pT_done"), sem("pT_ready"), sem("pv_done"), sem("oh_ready"), sem("ol_ready")
        lg_done, top_ready, gexp_ready, sel_ready, pos_done, routed = (sem(n) for n in (
            "lg_done", "top_ready", "gexp_ready", "sel_ready", "pos_done", "routed"))
        hrow_done, hrow_ready = sem("hrow_done"), sem("hrow_ready")
        msilu_done, gum_ready, t_done, th_ready, tl_ready = (sem(n) for n in ("msilu_done", "gum_ready", "t_done", "th_ready", "tl_ready"))
        P_ready, gath_done, xh_ready, xl_ready, slots_done, si_ready, PT_ready = (sem(n) for n in (
            "P_ready", "gath_done", "xh_ready", "xl_ready", "slots_done", "si_ready", "PT_ready"))
        scat_done, y_added, yh_ready, yl_ready, stepped = (sem(n) for n in ("scat_done", "y_added", "yh_ready", "yl_ready", "stepped"))

        block = ctx.enter_context(nc.Block())

        @block.sync
        def _(sp):
            def load(q, src, k, r=0):
                if q >= NRAW:
                    sp.wait_ge(lo_ready, r * NRAW + (q - NRAW + 1))
                if not isinstance(r, int):
                    sp.sem_inc(slots_freed, 1)
                sp.dma_start(raw[:, q % NRAW, :].rearrange("p (k n) -> p k n", k=k), src).then_inc(raw_loaded[q % NRAW], 16)

            def columns(w, u):
                return w[:, 256 * u:256 * u + 256].rearrange("(k p) n -> p k n", p=P)

            def expert(e, n, r=0):
                kind, b = SEQ[n // 2]
                one, h = bass.ds(e, 1), n % 2
                if kind == "d":
                    a = 512 * b + 256 * h
                    load(Q_MOE + n, A["w2_moe"][one, a:a + 256, :].rearrange("a (f p) n -> p (a f) n", p=P), 2, r)
                else:
                    w = A["w1_moe" if kind == "g" else "w3_moe"]
                    load(Q_MOE + n, w[one, 512 * h:512 * h + 512, 512 * b:512 * b + 512].rearrange("a (k p) n -> p (a k) n", p=P), 4, r)

            def embedding(layer, q, r=0):
                load(q, A["w_ple_proj"][layer].rearrange("(k p) n -> p k n", p=P), 2, r)
                for u in range(4):
                    load(q + 1 + u, columns(A["w_ple_gate"][layer], u), KC, r)

            sp.dma_start(vec[:, :, :], A["vec"]).then_inc(vec_loaded, 16)
            sp.dma_start(xT[:, :, :], A["xT"].rearrange("(k p) t -> p k t", p=P)).then_inc(x_loaded, 16)
            load(Q_POOL, A["w_pool"].rearrange("g (c p) n -> p (g c) n", p=P), KC)
            for n in range(2 * 3 - 1):
                load(Q_UP + n, columns(A["w3_dense" if n % 2 else "w1_dense"], n // 2), KC)
            w13 = [A[w].rearrange("(k p) n -> p k n", p=P) for w in ("w1_dense", "w3_dense")]
            with sp.Fori(0, 3) as i:
                for n in range(5, 11):
                    load(Q_UP + n, w13[n % 2][:, :, bass.ds(i * 768 + 256 * (n // 2), 256)], KC, i)
            for n in range(23, 2 * NUP):
                load(Q_UP + n, columns(A["w3_dense" if n % 2 else "w1_dense"], n // 2), KC)
            w2 = A["w2_dense"].rearrange("(u f p) n -> u p f n", p=P, f=2)
            for d in range(2):
                load(Q_DOWN + d, w2[d], 2)
            with sp.Fori(0, 2) as i:
                for d in range(2, 8):
                    load(Q_DOWN + d, w2[bass.ds(i * 6 + d, 1)].rearrange("u p f n -> p (u f) n"), 2, i)
            embedding(0, Q_PROJ)
            load(Q_K, A["w_k"].rearrange("(k p) n -> p k n", p=P), KC)
            load(Q_V, A["w_v"].rearrange("(k p) n -> p k n", p=P), KC)
            sp.wait_ge(pl_ready, 1)
            sp.dma_start(pT[:, :].rearrange("p (k t) -> p k t", k=2), A["pT"][1].rearrange("(k p) t -> p k t", p=P)).then_inc(p_loaded, 16)
            for w, q in (("w_q", Q_Q), ("w_o", Q_O)):
                for u in range(4):
                    load(q + u, columns(A[w], u), KC)
            sp.wait_ge(k_ready, 2)
            sp.wait_ge(v_ready, 2)
            sp.wait_ge(cache_loaded, 32)
            sp.dma_start(A["kT_prompt"].rearrange("(a p) t -> p a t", p=P), kTt[:, :, TP - 128:TP]).then_inc(kv_stored, 16)
            sp.dma_start(A["kT_sample"].rearrange("(a p) t -> p a t", p=P), kTt[:, :, TP + 64:TP + 192]).then_inc(kv_stored, 16)
            sp.dma_start(A["v_prompt"], vv[:, 1, :]).then_inc(kv_stored, 16)
            sp.dma_start(A["v_sample"][0:64], vv[64:128, 3, :]).then_inc(kv_stored, 16)
            sp.dma_start(A["v_sample"][64:128], vv[0:64, 2, :]).then_inc(kv_stored, 16)
            for n in range(NRAW):
                expert(0, n)
            sp.wait_ge(routed, 1)
            m = sp.value_load(extra[0:1, 0:1], min_val=0, max_val=2)
            with sp.Fori(0, m * NE + (NE - 1)) as i:
                for n in range(NRAW, NU):
                    expert(i % NE, n, i * RND)
                for n in range(NRAW):
                    kind, b = SEQ[n // 2]
                    w, h = A["w1_moe" if kind == "g" else "w3_moe"], n % 2
                    load(Q_MOE + NU + n, w[bass.ds((i + 1) % NE, 1), 512 * h:512 * h + 512, 512 * b:512 * b + 512]
                         .rearrange("a (k p) n -> p (a k) n", p=P), 4, i * RND)
            last = m * (NE * RND) + (NE - 1) * RND
            for n in range(NRAW, NU):
                expert(NE - 1, n, last)
            embedding(1, Q_MOE + NU, last)
            yo = A["yT"].rearrange("(k p) t -> p k t", p=P)
            for c in range(0, KC, 2):
                sp.wait_ge(h_ready, 7 * KC + c + 2)
                sp.dma_start(yo[:, c:c + 2, :], hT[:, c:c + 2, :]).then_inc(y_stored, 16)
            sp.wait_ge(pool_stored, 32)
            sp.wait_ge(kv_stored, 80)
            sp.wait_ge(y_stored, 64)

        @block.gpsimd
        def _(pool):
            pool.memset(ones[:, :], 1.0).then_inc(consts, 1)
            pool.memset(eps[:, :], EPS).then_inc(consts, 1)
            pool.memset(hcat[:, :, 0:HIST], 0.0).then_inc(hzero, 1)
            pool.dma_start(hcat[:, :, PADS - HIST:PADS], A["histT"].rearrange("(k p) t -> p k t", p=P)).then_inc(hist_loaded, 16)
            pool.iota(iota_i[:, :], pattern=[[1, 16]], base=1, channel_multiplier=0).then_inc(consts, 1)
            pool.iota(iota[:, :], pattern=[[1, T]], base=0, channel_multiplier=0,
                      allow_small_or_imprecise_dtypes=True).then_inc(consts, 1)
            pool.iota(tg[:, :, 0], pattern=[[P, 3]], base=0, channel_multiplier=1,
                      allow_small_or_imprecise_dtypes=True).then_inc(consts, 1)
            pool.wait_ge(consts, 5)
            pool.affine_select(out=ident[:, :], in_=ones[:, :], compare_op=ALU.is_equal, fill=0.0, base=0,
                               pattern=[[-1, P]], channel_multiplier=1).then_inc(consts, 1)
            pool.affine_select(out=tri[:, :], in_=ones[:, :], compare_op=ALU.is_gt, fill=0.0, base=0,
                               pattern=[[1, P]], channel_multiplier=-1).then_inc(consts, 1)
            pool.memset(mask[:, :], 0.0).then_inc(consts, 1)
            pool.wait_ge(consts, 8)
            pool.tensor_copy(identb[:, :], ident[:, :]).then_inc(consts, 1)
            pool.wait_ge(consts, 9)
            pool.memset(mask[0:64, 192:256], NEG).then_inc(consts, 1)
            pool.wait_ge(consts, 10)
            pool.memset(mask[64:128, 0:64], NEG).then_inc(consts, 1)
            pool.wait_ge(consts, 11)
            pool.memset(mask[0:64, 320:384], NEG).then_inc(consts, 1)
            pool.wait_ge(hcat_ready, 16)
            for name, a in (("poolT_prompt", PADP + TP - HIST), ("poolT_sample", PADS + TS - HIST)):
                pool.dma_start(A[name].rearrange("(k p) t -> p k t", p=P), hcat[:, :, a:a + HIST]).then_inc(pool_stored, 16)
        NCONST = 12

        @block.scalar
        def _(act):
            act.dma_start(rows[0:1, :], A["rows"]).then_inc(small_loaded, 16)
            act.dma_start(sinks[:, :], A["sinks"]).then_inc(small_loaded, 16)
            act.dma_start(wr[:, :, :], A["w_router"].rearrange("(k p) n -> p k n", p=P)).then_inc(small_loaded, 16)
            act.dma_start(pT[:, :].rearrange("p (k t) -> p k t", k=2), A["pT"][0].rearrange("(k p) t -> p k t", p=P)).then_inc(p_loaded, 16)
            act.sem_inc(silu_done, 2)

            def hi(q, r=0):
                act.wait_ge(raw_loaded[q % NRAW], r * 16 + 16 * (q // NRAW + 1))
                if q >= NSPL:
                    act.wait_ge(unit_done, r * NRAW + (q - NSPL + 1))
                nc.scalar.activation(Sh[:, q % NSPL, :], raw[:, q % NRAW, :], ACT.Copy).then_inc(hi_ready, 1)

            def squares(k, c0, c1):
                for c in range(c0, c1):
                    act.wait_ge(x_ready, KC * (k - 1) + c + 1)
                    nc.scalar.activation(sq3[:, c, :], xT[:, c, :], ACT.Square).then_inc(sq_ready, 1)

            def root(k):
                act.wait_ge(stat_done, k + 1)
                nc.scalar.activation(std[:, :], PS[:, 7, 0:T], ACT.Sqrt, bias=eps[:, :], scale=1.0 / D).then_inc(std_ready, 1)

            def high_h(s):
                for c in range(KC):
                    act.wait_ge(h_ready, KC * (s + (s == 5)) + c + 1)
                    nc.scalar.activation(Ah3[:, c, :], hT[:, c, :], ACT.Copy).then_inc(hh_ready, 1)

            hi(0)
            act.wait_ge(consts, NCONST)
            act.wait_ge(x_loaded, 16)
            for c in range(KC):
                nc.scalar.activation(sq3[:, c, :], xT[:, c, :], ACT.Square).then_inc(sq_ready, 1)
            root(0)
            hi(1)
            hi(2)
            act.wait_ge(vec_loaded, 16)
            high_h(0)
            hi(3)
            squares(1, 0, KC)
            root(1)
            high_h(1)

            def silu(r, b):
                act.wait_ge(unit_done, r * 6 + (Q_UP + 2 * b + 1))
                act.wait_ge(gu_ready, r * 6 + (2 * b + 2))
                for f in range(2):
                    nc.scalar.activation(sg[:, f, :], PS[:, f, 0:T], ACT.Silu).then_inc(silu_done, 1)

            def high_gu(d, src):
                o = GUOFF[d % 3]
                nc.scalar.activation(view(Ah, o, 2 * T), src, ACT.Copy).then_inc(gh_ready, 1)

            with act.Fori(0, 4) as i:
                for j in range(6):
                    if j % 2 == 0:
                        silu(i, j // 2)
                    hi(Q_UP + j + NSPL, i)
            silu(0, 12)
            hi(28)
            hi(29)
            high_gu(0, G[:, 0:2 * T])
            silu(0, 13)
            hi(30)
            act.wait_ge(gu_ready, 2 * NUP + 2)
            act.wait_ge(unit_done, Q_DOWN)
            high_gu(1, G[:, 2 * T:4 * T])
            with act.Fori(0, 2) as i:
                for d in range(2, 8):
                    act.wait_ge(unit_done, i * 6 + (Q_DOWN + d - 2))
                    high_gu(d, G[:, bass.ds(i * (12 * T) + 2 * T * d, 2 * T)])
                    hi(Q_DOWN + d, i)

            hi(Q_PROJ)
            hi(Q_PROJ + 1)
            act.wait_ge(p_loaded, 16)
            nc.scalar.activation(view(Ah, KC * T, 2 * T), pT[:, :], ACT.Copy).then_inc(ph_ready, 1)
            hi(Q_PROJ + 2)

            def gate_phase(layer, k, s, q, r, ahead):
                squares(k, 0, KC)
                root(k)
                high_h(s)
                for c in range(KC):
                    if c == 0:
                        act.wait_ge(unit_done, r * NRAW + (q + 1))
                        hi(q + 3, r)
                    nc.scalar.activation(ep3[:, c, :], PS[:, c, 0:T], ACT.Copy).then_inc(eple_ready, 1)
                for u in range(4):
                    act.wait_ge(unit_done, r * NRAW + (q + 2 + u))
                    for c in (2 * u, 2 * u + 1):
                        if c >= 2:
                            act.wait_ge(x_ready, KC * k + c - 1)
                        nc.scalar.activation(sig[:, c % 2, :], PS[:, c, 0:T], ACT.Sigmoid).then_inc(sig_ready, 1)
                    if ahead or u == 0:
                        hi(q + 4 + u, r)
                    if u:
                        squares(k + 1, 2 * u - 2, 2 * u)
                squares(k + 1, KC - 2, KC)
                root(k + 1)

            gate_phase(0, 2, 2, Q_PROJ, 0, True)
            high_h(3)
            act.dma_start(kTt[:, :, TP:TP + 128], A["cache_kT"].rearrange("(a p) t -> p a t", p=P)).then_inc(cache_loaded, 16)
            act.dma_start(vv[:, 3, :], A["cache_v"]).then_inc(cache_loaded, 16)
            act.wait_ge(unit_done, Q_K + 1)
            for a in range(2):
                nc.scalar.activation(kTt[:, a, 0:TP], PS[:, 4 + a, 0:TP], ACT.Identity, bias=vec[:, B_K, a:a + 1])
                nc.scalar.activation(kTt[:, a, TP + 128:NKEY], PS[:, 4 + a, TP:T], ACT.Identity,
                                     bias=vec[:, B_K, a:a + 1]).then_inc(k_ready, 1)
            hi(Q_K + 3)
            act.wait_ge(unit_done, Q_V + 1)
            high_h(4)
            for a in range(2):
                nc.scalar.activation(vT[:, a, :], PS[:, 6 + a, 0:T], ACT.Identity, bias=vec[:, B_V, a:a + 1]).then_inc(vT_ready, 1)
            hi(Q_V + 3)
            def query(u):
                act.wait_ge(unit_done, Q_Q + u + 1)
                for c in (2 * u, 2 * u + 1):
                    nc.scalar.activation(qT[:, c, :], PS[:, QBANK[u] + c % 2, 0:T], ACT.Identity, bias=vec[:, B_Q, c:c + 1]).then_inc(q_ready, 1)
                hi(Q_Q + u + 3)

            def exps(j):
                b0, o = 2 * (j % 2), 25 * (j % 2)
                neg, acc = st[:, o + 5:o + 10], st[:, o + 15:o + 20]
                act.wait_ge(max_ready, j + 1)
                if j >= 2:
                    act.wait_ge(pT_done, 2 * j - 2)
                for h in range(2):
                    nc.scalar.activation(pp[:, b0 + h, 0:256], PS[:, b0 + h, 0:256], ACT.Exp, scale=0.125,
                                         bias=neg[:, h:h + 1], accum_out=acc[:, h:h + 1])
                    nc.scalar.activation(pp[:, b0 + h, 256:384], PS[:, b0 + h, 256:384], ACT.Exp, scale=0.125,
                                         bias=neg[:, 2 + h:3 + h], accum_out=acc[:, 2 + h:3 + h])
                nc.scalar.activation(psm[:, j % 2, 0:192].rearrange("p (b n) -> p b n", b=2), PS[:, b0:b0 + 2, 384:480], ACT.Exp,
                                     scale=0.125, bias=neg[:, 4:5], accum_out=acc[:, 4:5])
                nc.scalar.activation(st[:, o + 20:o + 25], st[:, o + 10:o + 15], ACT.Exp).then_inc(exp_done, 1)

            def high_o(j):
                act.wait_ge(pv_done, j + 1)
                nc.scalar.activation(Ah3[:, j, :], PS[:, PVBANK[j % 2], 0:T], ACT.Copy).then_inc(oh_ready, 1)

            query(0)
            query(1)
            query(2)
            exps(0)
            exps(1)
            query(3)
            for j in range(KC):
                if 1 <= j < KC - 1:
                    exps(j + 1)
                if j >= 2:
                    act.wait_ge(pv_done, j - 1)
                for n in range(2):
                    act.wait_ge(pT_done, 2 * j + n + 1)
                    nc.scalar.activation(pTr[:, 2 * (j % 2) + n, :], PS[:, 5 + n, :], ACT.Copy).then_inc(pT_ready, 1)
                if j:
                    high_o(j - 1)
            high_o(KC - 1)
            for u in range(4):
                hi(Q_O + u + 3)
                squares(4, 2 * u, 2 * u + 2)
            root(4)
            act.wait_ge(top_ready, 1)
            nc.scalar.activation(rt[:, :, 1], rt[:, :, 0], ACT.Exp).then_inc(gexp_ready, 1)
            act.wait_ge(kv_stored, 80)
            for n in range(6):
                act.wait_ge(hrow_done, n + 1)
                t, half = n // 2, n % 2
                r = TS if t == 2 else P
                nc.scalar.activation(hrow[0:r, t, 512 * half:512 * half + 512], PS[0:r, 2 + n % 4, :], ACT.Copy).then_inc(hrow_ready, 1)

            def high_x(hf, count):
                act.wait_ge(gath_done, count)
                nc.scalar.activation(view(Ah, 512 * hf, 512), PS[:, 1 + 3 * hf, :], ACT.Copy).then_inc(xh_ready, 1)

            high_x(0, 1)
            high_x(1, 2)
            act.wait_ge(routed, 1)
            m = act.value_load(extra[0:1, 0:1], min_val=0, max_val=2)
            with act.Fori(0, m * NE + NE) as i:
                def high_t(b):
                    act.wait_ge(t_done, i * NBK + (b + 1))
                    nc.scalar.activation(view(Ah, 1024 + 512 * (b % 2), 512), PS[:, 0, :], ACT.Copy).then_inc(th_ready, 1)

                for n in range(NU):
                    kind, b = SEQ[n // 2]
                    if n % 2 and kind == "g":
                        act.wait_ge(unit_done, i * NU + (Q_MOE + n + 1))
                        nc.scalar.activation(sgm[:, b % 2, :], PS[:, 2 + 2 * (b % 2), :], ACT.Silu).then_inc(msilu_done, 1)
                    if n % 2 == 0 and kind == "u" and b:
                        high_t(b - 1)
                    if n == NU - 3:
                        high_t(NBK - 1)
                        high_x(0, i * 2 + 3)
                        high_x(1, i * 2 + 4)
                    if n == NU - 1:
                        act.wait_ge(unit_done, i * NU + (Q_MOE + NU))
                        for hf in range(2):
                            nc.scalar.activation(ysh[:, 512 * hf:512 * hf + 512], PS[:, 6 + hf, :], ACT.Copy,
                                                 scale=si[:, 1:2]).then_inc(yh_ready, 1)
                    hi(Q_MOE + n + NSPL, i * RND)
            end = m * (NE * RND) + (NE - 1) * RND
            act.wait_ge(p_loaded, 32)
            act.wait_ge(y_added, m * (NE * KC) + (NE * KC + KC))
            nc.scalar.activation(view(Ah, KC * T, 2 * T), pT[:, :], ACT.Copy).then_inc(ph_ready, 1)
            gate_phase(1, 5, 5, Q_MOE + NU, end, False)

        @block.tensor
        def _(pe):
            def mm(out, w, m, start, stop, **kw):
                return nc.tensor.matmul(out, w, m, start=start, stop=stop, **kw)

            def mm3(out, wh, wl, xh, xl, start, stop, **kw):
                mm(out, wh, xh, start, False, **kw)
                mm(out, wh, xl, False, False, **kw)
                return mm(out, wl, xh, False, stop, **kw)

            def unit(q, k, r=0):
                pe.wait_ge(lo_ready, r * NRAW + (q + 1))
                return (s[:, q % NSPL, :].rearrange("p (k n) -> p k n", k=k) for s in (Sh, Sl))

            def dense(out, wh, wl, c, xh, xl):
                for k in range(KC):
                    last = mm3(out, wh[:, k, P * c:P * c + P], wl[:, k, P * c:P * c + P], xh[:, k, :], xl[:, k, :], k == 0, k == KC - 1)
                return last

            pe.wait_ge(consts, NCONST)

            def norm(k):
                for c in range(KC):
                    pe.wait_ge(sq_ready, KC * k + c + 1)
                    last = mm(PS[:, 7, 0:T], ones[:, :], sq3[:, c, :], c == 0, c == KC - 1)
                last.then_inc(stat_done, 1)

            norm(0)
            wh, wl = unit(Q_POOL, KC)
            for c in range(KC):
                g, o = c // 2, P * (c % 2)
                pe.wait_ge(hl_ready, 2 * g + 2)
                for i in (2 * g, 2 * g + 1):
                    last = mm3(PS[:, 7 - c, 0:T], wh[:, i, o:o + P], wl[:, i, o:o + P], Ah3[:, i, :], Al3[:, i, :], i == 2 * g, i == 2 * g + 1)
                if c == KC - 1:
                    last.then_inc(unit_done, 1)
            norm(1)
            pe.wait_ge(hl_ready, 2 * KC)

            def up_unit(j, r=0):
                wh, wl = unit(Q_UP + j, KC, r)
                b = j // 2
                if j % 2 == 0:
                    pe.wait_ge(silu_done, r * 6 + (2 * b + 2))
                else:
                    pe.wait_ge(gu_ready, r * 6 + (2 * b + 2))
                for f in range(2):
                    last = dense(PS[:, 2 * (j % 2) + f, 0:T], wh, wl, f, Ah3, Al3)
                last.then_inc(unit_done, 1)

            with pe.Fori(0, 4) as i:
                for j in range(6):
                    up_unit(j, i)
            for j in range(24, 2 * NUP):
                up_unit(j)

            def down_unit(d, r=0):
                wh, wl = unit(Q_DOWN + d, 2, r)
                pe.wait_ge(gl_ready, r * 6 + (d + 1))
                o = GUOFF[d % 3]
                gh, gl = view(Ah, o, 2 * T, 2), view(Al, o, 2 * T, 2)
                for f in range(2):
                    for c in range(KC):
                        if d == 0 and f == 0 and c == 4:
                            pe.wait_ge(gu_ready, 2 * NUP + 2)
                        last = mm3(PS[:, 7 - c, 0:T], wh[:, f, P * c:P * c + P], wl[:, f, P * c:P * c + P], gh[:, f, :], gl[:, f, :],
                                   d == 0 and f == 0, True, skip_group_check=True)
                last.then_inc(unit_done, 1)

            down_unit(0)
            down_unit(1)
            with pe.Fori(0, 2) as i:
                for d in range(2, 8):
                    down_unit(d, i)

            def gate_phase(layer, k, s, q, r):
                norm(k)
                wh, wl = unit(q, 2, r)
                pe.wait_ge(pl_ready, layer + 1)
                for c in range(KC):
                    if c == KC - 1:
                        pe.wait_ge(std_ready, k + 1)
                    for i in range(2):
                        last = mm3(PS[:, c, 0:T], wh[:, i, P * c:P * c + P], wl[:, i, P * c:P * c + P], pAh[:, i, :], pAl[:, i, :], i == 0, i == 1)
                last.then_inc(unit_done, 1)
                pe.wait_ge(hl_ready, KC * (s + 1))
                for u in range(4):
                    wh, wl = unit(q + 1 + u, KC, r)
                    for f in range(2):
                        pe.wait_ge(eple_ready, KC * layer + 2 * u + f + 1)
                        last = dense(PS[:, 2 * u + f, 0:T], wh, wl, f, Ah3, Al3)
                    last.then_inc(unit_done, 1)
                pe.wait_ge(sig_ready, KC * (layer + 1))
                norm(k + 1)

            gate_phase(0, 2, 2, Q_PROJ, 0)
            pe.wait_ge(hl_ready, 4 * KC)
            pe.wait_ge(std_ready, 4)
            for q in (Q_K, Q_V):
                wh, wl = unit(q, KC)
                for a in range(2):
                    last = dense(PS[:, 4 + 2 * (q - Q_K) + a, 0:T], wh, wl, a, Ah3, Al3)
                last.then_inc(unit_done, 1)
            pe.wait_ge(hl_ready, 5 * KC)

            def scores(j):
                a, b0 = j // 4, 2 * (j % 2)
                for b in range(2):
                    bank, o = b0 + b, 64 * b
                    mm(PS[:, bank, 0:384], identb[:, :], mask[:, :], True, False, skip_group_check=True)
                    mm(PS[:, bank, 0:256], qT[o:o + 64, j, P:2 * P], kTt[o:o + 64, a, 0:TP], False, False, skip_group_check=True)
                    mm(PS[:, bank, 256:384], qT[o:o + 64, j, 0:P], kTt[o:o + 64, a, 0:P], False, True, skip_group_check=True)
                for b in range(2):
                    o = 64 * b
                    for half in range(2):
                        last = mm(PS[o:o + 64, b0 + half, 384:480], qT[o:o + 64, j, TP:T],
                                  kTt[o:o + 64, a, TP + 96 * half:TP + 96 * half + 96], True, True, skip_group_check=True)
                last.then_inc(score_done, 1)

            for u in range(4):
                wh, wl = unit(Q_Q + u, KC)
                if u == 3:
                    pe.wait_ge(cache_loaded, 32)
                    pe.wait_ge(q_ready, 2)
                    scores(0)
                    pe.wait_ge(q_ready, 4)
                    scores(1)
                    pe.wait_ge(v_ready, 3)
                for f in range(2):
                    last = dense(PS[:, QBANK[u] + f, 0:T], wh, wl, f, Ah3, Al3)
                last.then_inc(unit_done, 1)
                if u == 0:
                    pe.wait_ge(vT_ready, 2)
                    pe.wait_ge(k_ready, 2)
                    for t in range(3):
                        n = TS if t == 2 else P
                        for a in range(2):
                            o = 256 * (t % 2) + P * a
                            last = nc.tensor.transpose(PS[0:n, 4 + t // 2, o:o + P], vT[:, a, P * t:P * t + n], ident[:, :])
                    last.then_inc(vt_done, 1)
            pe.wait_ge(q_ready, KC)
            for j in range(KC):
                a = j // 4
                for n in range(2):
                    pe.wait_ge(p_ready, 2 * j + n + 1)
                    if j:
                        pe.wait_ge(pT_ready, 2 * j + n - 1)
                    for blk in range(4):
                        src = psm[:, j % 2, P * n:P * n + P] if blk == 3 else pp[:, 2 * (j % 2) + n, P * blk:P * blk + P]
                        last = nc.tensor.transpose(PS[:, 5 + n, P * blk:P * blk + P], src, ident[:, :])
                    last.then_inc(pT_done, 1)
                if j < KC - 2:
                    pe.wait_ge(exp_done, j + 1)
                    scores(j + 2)
                pe.wait_ge(pT_ready, 2 * j + 2)
                if j >= 2:
                    pe.wait_ge(ol_ready, j - 1)
                for b in range(2):
                    o, h, bank = 64 * b, 2 * (j % 2) + b, PVBANK[j % 2]
                    vc = 64 * (2 * a + b)
                    mm(PS[o:o + 64, bank, P:2 * P], vv[:, 0, vc:vc + 64], pTr[:, h, 0:P], True, False)
                    mm(PS[o:o + 64, bank, P:2 * P], vv[:, 1, vc:vc + 64], pTr[:, h, P:2 * P], False, True)
                    mm(PS[o:o + 64, bank, 0:P], vv[:, 0, vc:vc + 64], pTr[:, h, 2 * P:3 * P], True, True)
                    mm(PS[o:o + 64, bank, TP:T], vv[:, 3, vc:vc + 64], pTr[:, 2 * (j % 2), 384 + o:384 + o + 64], True, False)
                    last = mm(PS[o:o + 64, bank, TP:T], vv[0:64, 2, vc:vc + 64], pTr[0:64, 2 * (j % 2) + 1, 384 + o:384 + o + 64], False, True)
                last.then_inc(pv_done, 1)
            pe.wait_ge(ol_ready, KC)
            for u in range(4):
                wh, wl = unit(Q_O + u, KC)
                if u >= 2:
                    pe.wait_ge(x_ready, 3 * KC + 2 * u - 2)
                for f in range(2):
                    last = dense(PS[:, 2 * (u % 2) + f, 0:T], wh, wl, f, Ah3, Al3)
                last.then_inc(unit_done, 1)
            norm(4)
            pe.wait_ge(small_loaded, 48)
            pe.wait_ge(h_ready, 6 * KC)
            for t in range(3):
                n = TS if t == 2 else P
                out = PS[0:n, 0, 8 * t:8 * t + 8]
                for k in range(KC):
                    mm(out, hT[:, k, P * t:P * t + n], wr[:, k, :], k == 0, False)
                last = mm(out, ones[0:1, 0:n], rows[0:1, :], False, True)
            last.then_inc(lg_done, 1)
            for n in range(6):
                t, half = n // 2, n % 2
                r = TS if t == 2 else P
                if n >= 4:
                    pe.wait_ge(hrow_ready, n - 3)
                for q in range(4):
                    last = nc.tensor.transpose(PS[0:r, 2 + n % 4, P * q:P * q + P], hT[:, 4 * half + q, P * t:P * t + r], ident[:, :])
                last.then_inc(hrow_done, 1)
            pe.wait_ge(sel_ready, 1)
            for t in range(4):
                for s in range(min(t, 2) + 1):
                    w = tri if s == t else ones
                    last = mm(PS[:, 1, 8 * t:8 * t + 8], w[:, :], sel[:, s, :], s == 0, s == min(t, 2))
            last.then_inc(pos_done, 1)
            pe.wait_ge(hrow_ready, 6)

            def gather(hf):
                for c in range(4):
                    for t in range(3):
                        r = TS if t == 2 else P
                        last = mm(PS[:, 1 + 3 * hf, P * c:P * c + P], hrow[0:r, t, 512 * hf + P * c:512 * hf + P * c + P], Pm[0:r, t, :],
                                  t == 0, t == 2)
                last.then_inc(gath_done, 1)

            def slot_info():
                for t in range(3):
                    last = mm(PS[:, 5, 0:2], Pm[:, t, :], tg[:, t, :], t == 0, t == 2)
                last.then_inc(slots_done, 1)

            pe.wait_ge(P_ready, 1)
            gather(0)
            gather(1)
            slot_info()

            def scatter(c):
                mm(PS[:, 1, 0:T], ysh[:, P * c:P * c + P], PT[:, :], True, False)
                mm(PS[:, 1, 0:T], ysl[:, P * c:P * c + P], PT[:, :], False, True).then_inc(scat_done, 1)

            pe.wait_ge(routed, 1)
            m = pe.value_load(extra[0:1, 0:1], min_val=0, max_val=2)
            with pe.Fori(0, m * NE + NE) as i:
                def scatter_next(c):
                    if c == 0:
                        pe.wait_ge(yl_ready, i * 2 + 2)
                        pe.wait_ge(PT_ready, i + 1)
                    else:
                        pe.wait_ge(y_added, i * KC + c)
                    scatter(c)

                def up(kind, b, h):
                    n = POS[kind, b] + h
                    bank = 2 + 2 * (b % 2) + (kind == "u")
                    if kind == "g" and b == 0 and h == 0:
                        pe.wait_ge(xl_ready, i * 2 + 2)
                    if kind == "u" and b == 1 and h == 0:
                        pe.wait_ge(si_ready, i + 1)
                    if kind == "g" and b != 1 and h == 0:
                        pe.wait_ge(gum_ready, i * NBK + (b + 1 if b == 0 else b))
                    wh, wl = unit(Q_MOE + n, 4, i * RND)
                    for k in range(4):
                        if n < KC and k == 2:
                            scatter_next(n)
                        last = mm3(PS[:, bank, :], xgh[:, 4 * h + k, :], xgl[:, 4 * h + k, :], wh[:, k, :], wl[:, k, :],
                                   h == 0 and k == 0, h == 1 and k == 3)
                    last.then_inc(unit_done, 1)

                def transposes(b):
                    pe.wait_ge(gum_ready, i * NBK + (b + 2))
                    pe.wait_ge(tl_ready, i * NBK + (b + 1))
                    for q in range(4):
                        last = nc.tensor.transpose(PS[:, 0, P * q:P * q + P], gum[:, b % 2, P * q:P * q + P], ident[:, :])
                    last.then_inc(t_done, 1)

                def down(b, h):
                    if h == 0:
                        pe.wait_ge(tl_ready, i * NBK + (b + 2))
                    wh, wl = unit(Q_MOE + POS["d", b] + h, 2, i * RND)
                    for f in range(2):
                        for hf in range(2):
                            j = 4 * (b % 2) + 2 * h + f
                            last = mm3(PS[:, 6 + hf, :], gth[:, j, :], gtl[:, j, :], wh[:, f, 512 * hf:512 * hf + 512], wl[:, f, 512 * hf:512 * hf + 512],
                                       b == 0 and h == 0 and f == 0, b == NBK - 1 and h == 1 and f == 1)
                    last.then_inc(unit_done, 1)

                for kind, b in SEQ:
                    if kind == "u" and b:
                        transposes(b - 1)
                    if (kind, b) == ("d", NBK - 1):
                        transposes(NBK - 1)
                        pe.wait_ge(P_ready, i + 2)
                        gather(0)
                        gather(1)
                        slot_info()
                    for h in range(2):
                        if kind == "d":
                            down(b, h)
                        else:
                            up(kind, b, h)
            pe.wait_ge(yl_ready, m * (2 * NE) + (2 * NE + 2))
            pe.wait_ge(PT_ready, m * NE + (NE + 1))
            for c in range(KC):
                pe.wait_ge(y_added, m * (NE * KC) + (NE * KC + c))
                scatter(c)
            gate_phase(1, 5, 5, Q_MOE + NU, m * (NE * RND) + (NE - 1) * RND)

        @block.vector
        def _(v):
            links = [0]

            def link(ins):
                links[0] += 1
                ins.then_inc(chain, 1)
                v.wait_ge(chain, links[0])

            def lo(q, r=0):
                v.wait_ge(hi_ready, r * NRAW + (q + 1))
                nc.vector.tensor_tensor(Sl[:, q % NSPL, :], raw[:, q % NRAW, :], Sh[:, q % NSPL, :].bitcast(F32),
                                        ALU.subtract).then_inc(lo_ready, 1)

            def low(out, x, high, done):
                return nc.vector.tensor_tensor(out, x, high.bitcast(F32), ALU.subtract).then_inc(done, 1)

            def norm(k):
                v.wait_ge(std_ready, k + 1)
                link(nc.vector.reciprocal(rstd[:, :], std[:, :]))

            def low_h(s, c):
                v.wait_ge(hh_ready, KC * s + c + 1)
                low(Al3[:, c, :], hT[:, c, :], Ah3[:, c, :], hl_ready)

            def scaled(g, s=None):
                for c in range(KC):
                    nc.vector.scalar_tensor_tensor(out=hT[:, c, :], in0=xT[:, c, :], scalar=vec[:, g, c:c + 1], in1=rstd[:, :],
                                                   op0=ALU.mult, op1=ALU.mult).then_inc(h_ready, 1)
                    if s is not None and c:
                        low_h(s, c - 1)
                if s is not None:
                    low_h(s, KC - 1)

            v.sem_inc(gu_ready, 2)
            v.sem_inc(tl_ready, 1)
            v.sem_inc(gum_ready, 1)
            v.sem_inc(PT_ready, 1)
            v.sem_inc(yl_ready, 2)
            v.wait_ge(consts, NCONST)
            link(nc.vector.tensor_copy(st[:, 0:16], iota_i[:, :]))
            link(nc.vector.reciprocal(inv[:, :], st[:, 0:16]))
            v.wait_ge(vec_loaded, 16)
            lo(0)
            norm(0)
            for c in range(KC):
                for a, b, o in ((0, TP, PADP), (TP, T, PADS)):
                    nc.vector.scalar_tensor_tensor(out=hcat[:, c, o:o + b - a], in0=xT[:, c, a:b], scalar=vec[:, G_MIX0, c:c + 1],
                                                   in1=rstd[:, a:b], op0=ALU.mult, op1=ALU.mult).then_inc(hcat_ready, 1)
            v.wait_ge(hcat_ready, 16)
            v.wait_ge(hzero, 1)
            v.wait_ge(hist_loaded, 16)
            link(nc.vector.tensor_tensor(sA[:, :, 1:], hcat[:, :, 1:], hcat[:, :, 0:LCAT - 1], ALU.add))

            def diff(g, w, s):
                k = slice(2 * g, 2 * g + 2)
                link(nc.vector.tensor_tensor(s[:, k, PADP:PADP + w - 1], s[:, k, PADP:PADP + w - 1],
                                             inv[:, None, 0:w - 1].broadcast_to([P, 2, w - 1]), ALU.mult))
                nc.vector.tensor_tensor(hT[:, k, 0:w - 1], s[:, k, PADP:PADP + w - 1], hcat[:, k, PADP:PADP + w - 1], ALU.subtract)
                for o, a, n in ((PADP + w - 1, w - 1, TP - w + 1), (PADS, TP, TS)):
                    last = nc.vector.scalar_tensor_tensor(out=hT[:, k, a:a + n], in0=s[:, k, o:o + n], scalar=1.0 / w, in1=hcat[:, k, o:o + n],
                                                          op0=ALU.mult, op1=ALU.subtract)
                last.then_inc(h_ready, 2)

            link(nc.vector.tensor_tensor(sB[:, 2:, 3:], sA[:, 2:, 3:], sA[:, 2:, 1:LCAT - 2], ALU.add))
            diff(0, 2, sA)
            link(nc.vector.tensor_tensor(sA[:, 4:, 7:], sB[:, 4:, 7:], sB[:, 4:, 3:LCAT - 4], ALU.add))
            diff(1, 4, sB)
            low_h(0, 0)
            low_h(0, 1)
            link(nc.vector.tensor_tensor(sB[:, 6:, 15:], sA[:, 6:, 15:], sA[:, 6:, 7:LCAT - 8], ALU.add))
            diff(2, 8, sA)
            low_h(0, 2)
            low_h(0, 3)
            diff(3, 16, sB)
            for c in range(4, KC):
                low_h(0, c)
            lo(1)
            lo(2)
            v.wait_ge(unit_done, Q_POOL + 1)
            for c in range(KC):
                nc.vector.scalar_tensor_tensor(out=xT[:, c, :], in0=PS[:, 7 - c, 0:T], scalar=vec[:, POOL_SC, c:c + 1],
                                               in1=xT[:, c, :], op0=ALU.mult, op1=ALU.add).then_inc(x_ready, 1)
            lo(3)
            norm(1)
            scaled(G_FFN0, 1)
            v.wait_ge(pool_stored, 32)

            def glu_dense(r, b, out):
                v.wait_ge(silu_done, r * 6 + (2 * b + 4))
                v.wait_ge(unit_done, r * 6 + (Q_UP + 2 * b + 2))
                for f in range(2):
                    nc.vector.tensor_tensor(out(f), sg[:, f, :], PS[:, 2 + f, 0:T], ALU.mult).then_inc(gu_ready, 1)

            with v.Fori(0, 4) as i:
                for j in range(6):
                    if j % 2:
                        glu_dense(i, j // 2, lambda f: G[:, bass.ds(i * (6 * T) + (j // 2 * 2 + f) * T, T)])
                    lo(Q_UP + j + NSPL, i)

            def low_gu(d, src):
                low(view(Al, GUOFF[d % 3], 2 * T), src, view(Ah, GUOFF[d % 3], 2 * T), gl_ready)

            lo(28)
            glu_dense(0, 12, lambda f: guT[:, 24 + f, :])
            lo(29)
            v.wait_ge(gh_ready, 1)
            low_gu(0, G[:, 0:2 * T])
            lo(30)
            glu_dense(0, 13, lambda f: guT[:, 26 + f, :])
            v.wait_ge(gh_ready, 2)
            low_gu(1, G[:, 2 * T:4 * T])
            with v.Fori(0, 2) as i:
                for d in range(2, 8):
                    v.wait_ge(gh_ready, i * 6 + (d + 1))
                    low_gu(d, G[:, bass.ds(i * (12 * T) + 2 * T * d, 2 * T)])
                    lo(Q_DOWN + d, i)
            lo(Q_PROJ)
            lo(Q_PROJ + 1)
            v.wait_ge(ph_ready, 1)
            low(view(Al, KC * T, 2 * T), pT[:, :], view(Ah, KC * T, 2 * T), pl_ready)
            lo(Q_PROJ + 2)
            v.wait_ge(unit_done, Q_PROJ)
            for c in range(KC):
                nc.vector.tensor_tensor(xT[:, c, :], xT[:, c, :], PS[:, 7 - c, 0:T], ALU.add).then_inc(x_ready, 1)

            def gate_phase(layer, k, s, g, q, r, ahead):
                norm(k)
                scaled(g, s)
                lo(q + 3, r)
                for c in range(KC):
                    v.wait_ge(eple_ready, KC * layer + c + 1)
                    v.wait_ge(sig_ready, KC * layer + c + 1)
                    link(nc.vector.tensor_tensor(gtm[:, c % 2, :], sig[:, c % 2, :], ep3[:, c, :], ALU.mult))
                    nc.vector.tensor_tensor(xT[:, c, :], xT[:, c, :], gtm[:, c % 2, :], ALU.add).then_inc(x_ready, 1)
                    if c % 2 and (ahead or c == 1):
                        lo(q + 4 + c // 2, r)

            gate_phase(0, 2, 2, G_PLE0, Q_PROJ, 0, True)
            norm(3)
            scaled(G_KV, 3)
            lo(Q_K + 3)
            v.wait_ge(unit_done, Q_V + 1)
            scaled(G_MIX1, 4)
            lo(Q_V + 3)
            v.wait_ge(vt_done, 1)
            nc.vector.tensor_copy(vv[:, 0:2, :], PS[:, 4, :].rearrange("p (t n) -> p t n", t=2)).then_inc(v_ready, 1)
            nc.vector.tensor_copy(vv[0:TS, 2, :], PS[0:TS, 5, 0:256]).then_inc(v_ready, 1)
            nc.vector.memset(psm[:, :, 192:256], 0.0).then_inc(v_ready, 1)
            for u in range(3):
                lo(Q_Q + u + 3)
            v.wait_ge(small_loaded, 48)

            def maxima(j):
                b0, o = 2 * (j % 2), 25 * (j % 2)
                mx, neg, ds_ = (st[:, o + 5 * i:o + 5 * i + 5] for i in range(3))
                v.wait_ge(score_done, j + 1)
                nc.vector.reduce_max(mx[:, 0:2], PS[:, b0:b0 + 2, 0:256], AX.X)
                nc.vector.reduce_max(mx[:, 2:4], PS[:, b0:b0 + 2, 256:384], AX.X)
                link(nc.vector.reduce_max(mx[:, 4:5], PS[:, b0:b0 + 2, 384:480], AX.XY))
                link(nc.vector.scalar_tensor_tensor(out=mx, in0=mx, scalar=0.125, in1=sinks[:, 5 * j:5 * j + 5], op0=ALU.mult, op1=ALU.max))
                nc.vector.tensor_scalar(neg, mx, -1.0, None, ALU.mult)
                nc.vector.tensor_tensor(ds_, sinks[:, 5 * j:5 * j + 5], mx, ALU.subtract).then_inc(max_ready, 1)

            def probabilities(j):
                b0, o = 2 * (j % 2), 25 * (j % 2)
                acc, es = st[:, o + 15:o + 20], st[:, o + 20:o + 25]
                v.wait_ge(exp_done, j + 1)
                link(nc.vector.tensor_tensor(acc, acc, es, ALU.add))
                link(nc.vector.reciprocal(acc, acc))
                nc.vector.tensor_scalar(psm[:, j % 2, 0:192], psm[:, j % 2, 0:192], acc[:, 4:5], None, ALU.mult)
                for h in range(2):
                    nc.vector.tensor_scalar(pp[:, b0 + h, 0:256], pp[:, b0 + h, 0:256], acc[:, h:h + 1], None, ALU.mult)
                    nc.vector.tensor_scalar(pp[:, b0 + h, 256:384], pp[:, b0 + h, 256:384], acc[:, 2 + h:3 + h], None, ALU.mult).then_inc(p_ready, 1)

            def low_o(j):
                v.wait_ge(oh_ready, j + 1)
                low(Al3[:, j, :], PS[:, PVBANK[j % 2], 0:T], Ah3[:, j, :], ol_ready)

            maxima(0)
            maxima(1)
            probabilities(0)
            probabilities(1)
            lo(Q_Q + 6)
            for j in range(1, KC):
                if j < KC - 1:
                    maxima(j + 1)
                    probabilities(j + 1)
                low_o(j - 1)
            low_o(KC - 1)
            for u in range(4):
                v.wait_ge(unit_done, Q_O + u + 1)
                for c in (2 * u, 2 * u + 1):
                    nc.vector.tensor_tensor(xT[:, c, :], xT[:, c, :], PS[:, c % 4, 0:T], ALU.add).then_inc(x_ready, 1)
                lo(Q_O + u + 3)
            norm(4)
            scaled(G_FFN1)
            v.wait_ge(kv_stored, 80)
            for z in (lg[:, :, :], gate[:, :, :], sel[:, :, :], ysh.bitcast(F32), ysl.bitcast(F32), PT[:, :].bitcast(F32)):
                nc.vector.memset(z, 0.0).then_inc(chain, 1)
                links[0] += 1
            v.wait_ge(chain, links[0])
            v.wait_ge(lg_done, 1)
            nc.vector.tensor_copy(lg[:, 0:2, :], PS[:, 0, 0:16].rearrange("p (t e) -> p t e", t=2))
            link(nc.vector.tensor_copy(lg[0:TS, 2, :], PS[0:TS, 0, 16:24]))
            for t in range(3):
                link(nc.vector.max(top[:, t, :], lg[:, t, :]))
                link(nc.vector.max_index(topi[:, t, :], top[:, t, :], lg[:, t, :]))
            nc.vector.tensor_tensor(rt[:, :, 0], top[:, :, 1], top[:, :, 0], ALU.subtract).then_inc(top_ready, 1)
            link(nc.vector.tensor_copy(rt[:, :, 2:4], topi[:, :, 0:2]))
            v.wait_ge(gexp_ready, 1)
            link(nc.vector.tensor_scalar(rt[:, :, 0], rt[:, :, 1], 1.0, None, ALU.add))
            link(nc.vector.reciprocal(rt[:, :, 0], rt[:, :, 0]))
            link(nc.vector.tensor_tensor(rt[:, :, 1], rt[:, :, 1], rt[:, :, 0], ALU.mult))
            for t in range(3):
                r = TS if t == 2 else P
                nc.vector.tensor_scalar(sel[0:r, t, :], iota[0:r, 0:NE], rt[0:r, t, 2:3], None, ALU.is_equal)
                link(nc.vector.tensor_scalar(oh[0:r, t, :], iota[0:r, 0:NE], rt[0:r, t, 3:4], None, ALU.is_equal))
                link(nc.vector.tensor_scalar(gate[0:r, t, :], sel[0:r, t, :], rt[0:r, t, 0:1], None, ALU.mult))
                link(nc.vector.scalar_tensor_tensor(out=gate[0:r, t, :], in0=oh[0:r, t, :], scalar=rt[0:r, t, 1:2], in1=gate[0:r, t, :],
                                                    op0=ALU.mult, op1=ALU.add))
                link(nc.vector.tensor_tensor(sel[0:r, t, :], sel[0:r, t, :], oh[0:r, t, :], ALU.add))
            v.sem_inc(sel_ready, 1)
            v.wait_ge(pos_done, 1)
            link(nc.vector.scalar_tensor_tensor(out=posm[:, :, :], in0=PS[:, 1, 0:24].rearrange("p (t e) -> p t e", t=3), scalar=1.0,
                                                in1=sel[:, :, :], op0=ALU.add, op1=ALU.mult))
            nc.vector.tensor_scalar(posm[:, :, :], posm[:, :, :], -1.0, None, ALU.add).then_inc(stepped, 1)
            link(nc.vector.reduce_max(cnt[0:1, 0:1], PS[0:1, 1, 24:32], AX.X))
            nc.vector.tensor_scalar(cnt[0:1, 1:2], cnt[0:1, 0:1], float(P), None, ALU.is_gt)
            link(nc.vector.tensor_scalar(cnt[0:1, 2:3], cnt[0:1, 0:1], float(2 * P), None, ALU.is_gt))
            link(nc.vector.tensor_tensor(cnt[0:1, 3:4], cnt[0:1, 1:2], cnt[0:1, 2:3], ALU.add))
            nc.vector.tensor_copy(extra[0:1, 0:1], cnt[0:1, 3:4]).then_inc(routed, 1)

            def one_hots(e, steps):
                v.wait_ge(stepped, steps)
                for t in range(3):
                    nc.vector.tensor_scalar(Pm[:, t, :], iota[:, 0:P], posm[:, t, bass.ds(e, 1)], None, ALU.is_equal)
                nc.vector.tensor_copy(tg[:, :, 1:2], gate[:, :, bass.ds(e, 1)]).then_inc(P_ready, 1)
                v.wait_ge(P_ready, steps)
                nc.vector.tensor_scalar(posm[:, :, bass.ds(e, 1)], posm[:, :, bass.ds(e, 1)], float(-P), None, ALU.add).then_inc(stepped, 1)

            def low_x(hf, count):
                v.wait_ge(xh_ready, count)
                low(view(Al, 512 * hf, 512), PS[:, 1 + 3 * hf, :], view(Ah, 512 * hf, 512), xl_ready)

            def take_slots(count):
                v.wait_ge(slots_done, count)
                nc.vector.tensor_copy(si[:, :], PS[:, 5, 0:2]).then_inc(si_ready, 1)

            one_hots(0, 1)
            low_x(0, 1)
            low_x(1, 2)
            take_slots(1)
            v.wait_ge(routed, 1)
            m = v.value_load(extra[0:1, 0:1], min_val=0, max_val=2)

            def add_back(c, count):
                v.wait_ge(scat_done, count)
                nc.vector.tensor_tensor(xT[:, c, :], xT[:, c, :], PS[:, 1, 0:T], ALU.add).then_inc(y_added, 1)

            with v.Fori(0, m * NE + NE) as i:
                def low_t(b):
                    v.wait_ge(th_ready, i * NBK + (b + 1))
                    o = 1024 + 512 * (b % 2)
                    low(view(Al, o, 512), PS[:, 0, :], view(Ah, o, 512), tl_ready)

                for n in range(NU):
                    kind, b = SEQ[n // 2]
                    if n < KC:
                        add_back(n, i * KC + (n + 1))
                    if n == KC:
                        v.wait_ge(si_ready, i + 1)
                        nc.vector.tensor_scalar(PT[:, :], iota[:, :], si[:, 0:1], None, ALU.is_equal).then_inc(PT_ready, 1)
                    if n % 2 and kind == "u":
                        v.wait_ge(msilu_done, i * NBK + (b + 1))
                        v.wait_ge(unit_done, i * NU + (Q_MOE + n + 1))
                        nc.vector.tensor_tensor(gum[:, b % 2, :], sgm[:, b % 2, :], PS[:, 3 + 2 * (b % 2), :], ALU.mult).then_inc(gum_ready, 1)
                    if n % 2 == 0 and kind == "u" and b:
                        low_t(b - 1)
                    if n == NU // 2:
                        one_hots((i + 1) % NE, i + 2)
                    if n == NU - 3:
                        low_t(NBK - 1)
                        low_x(0, i * 2 + 3)
                        low_x(1, i * 2 + 4)
                    if n == NU - 1:
                        for hf in range(2):
                            v.wait_ge(yh_ready, i * 2 + (hf + 1))
                            nc.vector.scalar_tensor_tensor(out=ysl[:, 512 * hf:512 * hf + 512], in0=PS[:, 6 + hf, :], scalar=si[:, 1:2],
                                                           in1=ysh[:, 512 * hf:512 * hf + 512].bitcast(F32), op0=ALU.mult,
                                                           op1=ALU.subtract).then_inc(yl_ready, 1)
                        v.wait_ge(yl_ready, i * 2 + 4)
                        take_slots(i + 2)
                    lo(Q_MOE + n + NSPL, i * RND)
            for c in range(KC):
                add_back(c, m * (NE * KC) + (NE * KC + c + 1))
            v.wait_ge(ph_ready, 2)
            low(view(Al, KC * T, 2 * T), pT[:, :], view(Ah, KC * T, 2 * T), pl_ready)
            v.wait_ge(y_added, m * (NE * KC) + (NE * KC + KC))
            v.sem_inc(x_ready, KC)
            gate_phase(1, 5, 5, G_PLE1, Q_MOE + NU, m * (NE * RND) + (NE - 1) * RND, False)
            norm(6)
            scaled(G_FIN)


def kernel(**inputs):
    import numpy as np
    import concourse.bacc as bacc
    from concourse.bass_utils import run_bass_kernel_spmd as run

    a = {k: np.asarray(x) for k, x in inputs.items()}

    def chunks(x):
        return x.reshape(KC, P).T

    heads = [(2 * aa + b) * 4 + r for aa in range(2) for r in range(4) for b in range(2)]
    bq = a["b_q"][0].reshape(16, 64)[heads].reshape(KC, P).T
    bk = np.zeros((P, KC), a["b_k"].dtype)
    bk[:, 0:2] = a["b_k"].reshape(2, P).T
    bv = np.zeros((P, KC), a["b_v"].dtype)
    bv[:, 0:2] = a["b_v"].reshape(2, P).T
    vecs = [chunks(a["g_mix"][0]), chunks(a["g_ffn"][0]), chunks(a["g_ple"][0]), chunks(a["g_kv"]), chunks(a["g_mix"][1]),
            chunks(a["g_ffn"][1]), chunks(a["g_ple"][1]), chunks(a["g_final"]), chunks(a["pool_scale"][0]), bq, bk, bv]
    sk = a["sinks"][0]
    sink = np.zeros((P, 40), sk.dtype)
    for j in range(8):
        for b in range(2):
            sink[:, 5 * j + b] = sink[:, 5 * j + 2 + b] = sk[heads[2 * j + b]]
            sink[64 * b:64 * b + 64, 5 * j + 4] = sk[heads[2 * j + b]]
    ins = {
        "xT": np.concatenate([a["x_prompt"][0], a["x_sample"][0]], 0).T,
        "pT": np.concatenate([a["p_prompt"][:, 0], a["p_sample"][:, 0]], 1).transpose(0, 2, 1),
        "histT": a["state_pool"][0, 0].T,
        "vec": np.stack(vecs, 1),
        "rows": a["b_router"],
        "sinks": sink,
        "cache_kT": a["cache_k"][0].transpose(1, 2, 0).reshape(256, 128),
        "cache_v": a["cache_v"][0].reshape(128, 256),
        "w_pool": a["w_pool"][0], "w_k": a["w_k"], "w_v": a["w_v"],
        "w_q": a["w_q"][0].reshape(D, 16, 64)[:, heads].reshape(D, D),
        "w_o": a["w_o"][0].reshape(16, 64, D)[heads].reshape(D, D),
        "w1_dense": a["w1_dense"][0], "w3_dense": a["w3_dense"][0], "w2_dense": a["w2_dense"][0],
        "w_router": a["w_router"][0], "w1_moe": a["w1_moe"][0], "w3_moe": a["w3_moe"][0], "w2_moe": a["w2_moe"][0],
        "w_ple_proj": a["w_ple_proj"], "w_ple_gate": a["w_ple_gate"],
    }
    outs = {"yT": (D, T), "poolT_prompt": (D, HIST), "poolT_sample": (D, HIST), "kT_prompt": (256, 128), "kT_sample": (256, 128),
            "v_prompt": (128, 256), "v_sample": (128, 256)}
    nc = bacc.Bacc("TRN2", target_bir_lowering=False, num_devices=1)
    A, arrays = {}, {}
    for name, x in ins.items():
        arrays["in_" + name] = np.ascontiguousarray(x)
        A[name] = nc.dram_tensor("in_" + name, x.shape, mybir.dt.from_np(x.dtype), kind="ExternalInput").ap()
    for name, shape in outs.items():
        A[name] = nc.dram_tensor("out_" + name, shape, F32, kind="ExternalOutput").ap()
    build(nc, A)
    r = run(nc, [arrays], core_ids=[0]).results[0]
    o = {name: np.asarray(r["out_" + name]) for name in outs}
    y = o["yT"].T

    def keys(x):
        return np.ascontiguousarray(x.reshape(4, 64, 128).transpose(2, 0, 1))[None]

    return (np.ascontiguousarray(y[:TP])[None], np.ascontiguousarray(y[TP:])[None],
            np.ascontiguousarray(o["poolT_prompt"].T)[None, None], np.ascontiguousarray(o["poolT_sample"].T)[None, None],
            keys(o["kT_prompt"]), o["v_prompt"].reshape(1, 128, 4, 64), keys(o["kT_sample"]), o["v_sample"].reshape(1, 128, 4, 64))
```

```python
import concourse.bass as bass
from concourse import mybir
from contextlib import ExitStack

F32 = mybir.dt.float32
F32R = mybir.dt.float32r
BF16 = mybir.dt.bfloat16
I32 = mybir.dt.int32
U32 = mybir.dt.uint32
ALU = mybir.AluOpType
ACT = mybir.ActivationFunctionType
AX = mybir.AxisListType

P = 128
D, TP, TS = 1024, 256, 64
T = TP + TS
KC = D // P
FF = 3584
FC = FF // P
NE = 8
HIST = 15
PADP, PADS = HIST, HIST + TP + HIST
LCAT = PADS + TS
PLE = 256
NEG = -1e30
EPS = 1e-6
G_MIX0, G_FFN0, G_PLE0, G_KV, G_MIX1, G_FFN1, G_PLE1, G_FIN, POOL_SC, B_Q, B_K, B_V = range(12)
NVEC = 12

UNIT, NRAW, NSPL = 2048, 6, 3
Q_POOL = 0
Q_UP = 1
NUP = FF // 256
Q_DOWN = Q_UP + 2 * NUP
Q_PROJ = Q_DOWN + NUP
Q_GATE = Q_PROJ + 1
Q_K, Q_V = Q_GATE + 4, Q_GATE + 5
Q_Q = Q_V + 1
Q_O = Q_Q + 4
Q_MOE = Q_O + 4
NBK = 7
SEQ = [("g", 0), ("u", 0)]
for _b in range(1, NBK):
    SEQ += [("g", _b), ("u", _b), ("d", _b - 1)]
SEQ += [("d", NBK - 1)]
NU = 2 * len(SEQ)
POS = {s: 2 * n for n, s in enumerate(SEQ)}
QBANK = (0, 2, 6, 4)
PVBANK = (7, 4)
ORD = (0, 2, 3, 4, 1, 5, 6, 7)
assert POS["d", 0] == KC
assert NU % NRAW == 0 and NU % NSPL == 0 and NRAW % NSPL == 0
RND = NU // NRAW


def build(nc, A):
    ctx = ExitStack()
    with ctx:
        def sb(name, shape, dt=F32):
            return ctx.enter_context(nc.sbuf_tensor("s_" + name, shape, dt))

        def sem(name):
            return ctx.enter_context(nc.semaphore(name))

        PS = ctx.enter_context(nc.psum_tensor("PS", [P, 8, 512], F32))
        raw = sb("raw", [P, NRAW, UNIT])
        Sh, Sl = sb("Sh", [P, NSPL, UNIT], F32R), sb("Sl", [P, NSPL, UNIT], F32R)
        NA = 3072 + 2 * T
        Ah, Al = sb("Ah", [P, NA], F32R), sb("Al", [P, NA], F32R)
        G = sb("G", [P, FC * T])
        xT = sb("xT", [P, KC, T])
        hT = sb("hT", [P, KC, T])
        sq = sb("sq", [P, KC * T])
        pT = sb("pT", [P, 2 * T])
        vec = sb("vec", [P, NVEC, KC])
        std = sb("std", [P, T])
        rstd = sb("rstd", [P, T])
        spare = sb("spare", [P, 16])
        eps = sb("eps", [P, 1])
        ones = sb("ones", [P, P])
        ident = sb("ident", [P, P])
        tri = sb("tri", [P, P])
        identb = sb("identb", [P, P], BF16)
        mask = sb("mask", [P, 384], BF16)
        iota_i = sb("iota_i", [P, 16], I32)
        inv = sb("inv", [P, 16])
        iota = sb("iota", [P, T])
        wr = sb("wr", [P, KC, NE])
        br = sb("br", [NE, 1])
        lgT = sb("lgT", [NE, T])
        onesb = sb("onesb", [P, P], BF16)
        trib = sb("trib", [P, P], BF16)
        valid = sb("valid", [P, 3, NE])
        sinks = sb("sinks", [P, 40])
        st = sb("st", [P, 50])
        lg = sb("lg", [P, 3, NE])
        top = sb("top", [P, 3, NE])
        topi = sb("topi", [P, 3, NE], U32)
        rt = sb("rt", [P, 3, 4])
        oh = sb("oh", [P, 3, NE])
        gate = sb("gate", [P, 3, NE])
        eq = sb("eq", [P, 3, NE])
        sel = sb("sel", [P, 3, NE], BF16)
        posm = sb("posm", [P, 3, NE])
        tg = sb("tg", [P, 3, 2])
        si = sb("si", [P, 2])
        cnt = sb("cnt", [1, 4])
        extra = sb("extra", [1, 1], I32)
        PT = sb("PT", [P, T], F32R)

        def view(t, a, n, k=None):
            v = t[:, a:a + n]
            return v if k is None else v.rearrange("p (k n) -> p k n", k=k)

        sq3 = view(sq, 0, KC * T, KC)
        Ah3, Al3 = view(Ah, 0, KC * T, KC), view(Al, 0, KC * T, KC)
        PA = (KC * T, 3072)
        L8 = KC * LCAT
        hcat, sA, sB = view(G, 0, L8, KC), view(G, L8, L8, KC), view(G, 2 * L8, L8, KC)
        sg = view(sq, 0, 2 * T, 2)
        guT = view(G, 0, FC * T, FC)
        GUOFF = (KC * T, 0, 2 * T)
        sig, gtm, ep3 = view(G, 0, 2 * T, 2), view(G, 2 * T, 2 * T, 2), view(G, 4 * T, KC * T, KC)
        NKEY = TP + 128 + TS
        qT = view(G, 0, KC * T, KC)
        kTt = view(G, KC * T, 2 * NKEY, 2)
        vv = view(G, KC * T + 2 * NKEY, 1024, 4)
        pb0 = KC * T + 2 * NKEY + 1024
        pp = view(G, pb0, 4 * 384, 4)
        psm = view(G, pb0 + 4 * 384, 512, 2)
        vT = view(sq, 0, 2 * T, 2)
        pTr = view(sq, 0, 2048, 4)
        hrow = view(G, pb0, 3 * D, 3)
        sgm, gum = view(G, 0, 1024, 2), view(G, 1024, 1024, 2)
        Pm = view(G, 2048, 384, 3)
        xgh, xgl = view(Ah, 0, KC * P, KC), view(Al, 0, KC * P, KC)
        gth, gtl = view(Ah, 1024, 1024, 8), view(Al, 1024, 1024, 8)
        ysh, ysl = view(Ah, 2048, 1024), view(Al, 2048, 1024)

        x_loaded = [sem("x_loaded0"), sem("x_loaded1")]
        vec_loaded, small_loaded, hist_loaded, p_loaded, cache_loaded = (sem(n) for n in (
            "vec_loaded", "small_loaded", "hist_loaded", "p_loaded", "cache_loaded"))
        raw_loaded = [sem(f"raw_loaded{s}") for s in range(NRAW)]
        pool_stored, kv_stored, y_stored = sem("pool_stored"), sem("kv_stored"), sem("y_stored")
        hi_ready, lo_ready, unit_done = sem("hi_ready"), sem("lo_ready"), sem("unit_done")
        slots_freed = sem("slots_freed")
        sums_ready = sem("sums_ready")
        half_done, part_done, kv_left = sem("half_done"), sem("part_done"), sem("kv_left")
        consts, hzero, chain = sem("consts"), sem("hzero"), sem("chain")
        sq_ready, stat_done, std_ready, x_ready = sem("sq_ready"), sem("stat_done"), sem("std_ready"), sem("x_ready")
        h_ready, hh_ready, hl_ready, hcat_ready = sem("h_ready"), sem("hh_ready"), sem("hl_ready"), sem("hcat_ready")
        ph_ready, pl_ready = sem("ph_ready"), sem("pl_ready")
        silu_done, gu_ready, gh_ready, gl_ready = sem("silu_done"), sem("gu_ready"), sem("gh_ready"), sem("gl_ready")
        eple_ready, sig_ready = sem("eple_ready"), sem("sig_ready")
        k_ready, vT_ready, vt_done, v_ready, q_ready = (sem(n) for n in ("k_ready", "vT_ready", "vt_done", "v_ready", "q_ready"))
        score_done, max_ready, exp_done, p_ready = sem("score_done"), sem("max_ready"), sem("exp_done"), sem("p_ready")
        pT_done, pT_ready, pv_done, oh_ready, ol_ready = sem("pT_done"), sem("pT_ready"), sem("pv_done"), sem("oh_ready"), sem("ol_ready")
        lgT_done, lgT_ready = sem("lgT_done"), sem("lgT_ready")
        lg_done, top_ready, gexp_ready, sel_ready, pos_done, routed = (sem(n) for n in (
            "lg_done", "top_ready", "gexp_ready", "sel_ready", "pos_done", "routed"))
        hrow_done, hrow_ready = sem("hrow_done"), sem("hrow_ready")
        msilu_done, gum_ready, t_done, th_ready, tl_ready = (sem(n) for n in ("msilu_done", "gum_ready", "t_done", "th_ready", "tl_ready"))
        P_ready, gath_done, xh_ready, xl_ready, slots_done, si_ready, PT_ready = (sem(n) for n in (
            "P_ready", "gath_done", "xh_ready", "xl_ready", "slots_done", "si_ready", "PT_ready"))
        scat_done, y_added, yh_ready, yl_ready, stepped = (sem(n) for n in ("scat_done", "y_added", "yh_ready", "yl_ready", "stepped"))

        block = ctx.enter_context(nc.Block())

        @block.sync
        def _(sp):
            def load(q, src, k, r=0):
                if q >= NRAW:
                    sp.wait_ge(lo_ready, r * NRAW + (q - NRAW + 1))
                if not isinstance(r, int):
                    sp.sem_inc(slots_freed, 1)
                sp.dma_start(raw[:, q % NRAW, :].rearrange("p (k n) -> p k n", k=k), src).then_inc(raw_loaded[q % NRAW], 16)

            def columns(w, u):
                return w[:, 256 * u:256 * u + 256].rearrange("(k p) n -> p k n", p=P)

            def expert(e, n, r=0):
                kind, b = SEQ[n // 2]
                one, h = bass.ds(e, 1), n % 2
                if kind == "d":
                    a = 512 * b + 256 * h
                    load(Q_MOE + n, A["w2_moe"][one, a:a + 256, :].rearrange("a (f p) n -> p (a f) n", p=P), 2, r)
                else:
                    w = A["w1_moe" if kind == "g" else "w3_moe"]
                    load(Q_MOE + n, w[one, 512 * h:512 * h + 512, 512 * b:512 * b + 512].rearrange("a (k p) n -> p (a k) n", p=P), 4, r)

            def embedding(layer, q, r=0):
                load(q, A["w_ple_proj"][layer].rearrange("(k p) n -> p k n", p=P), 2, r)
                for u in range(4):
                    load(q + 1 + u, columns(A["w_ple_gate"][layer], u), KC, r)

            xin = A["xT"].rearrange("(k p) t -> p k t", p=P)
            for c in (0, 4):
                sp.dma_start(xT[:, c:c + 4, :], xin[:, c:c + 4, :]).then_inc(x_loaded[c // 4], 16)
            sp.dma_start(vec[:, :, :], A["vec"]).then_inc(vec_loaded, 16)
            load(Q_POOL, A["w_pool"].rearrange("g (c p) n -> p (g c) n", p=P), KC)
            for n in range(2 * 3 - 1):
                load(Q_UP + n, columns(A["w3_dense" if n % 2 else "w1_dense"], n // 2), KC)
            w13 = [A[w].rearrange("(k p) n -> p k n", p=P) for w in ("w1_dense", "w3_dense")]
            with sp.Fori(0, 3) as i:
                for n in range(5, 11):
                    load(Q_UP + n, w13[n % 2][:, :, bass.ds(i * 768 + 256 * (n // 2), 256)], KC, i)
            for n in range(23, 2 * NUP):
                load(Q_UP + n, columns(A["w3_dense" if n % 2 else "w1_dense"], n // 2), KC)
            w2 = A["w2_dense"].rearrange("(u f p) n -> u p f n", p=P, f=2)
            for d in range(2):
                load(Q_DOWN + d, w2[d], 2)
            with sp.Fori(0, 2) as i:
                for d in range(2, 8):
                    load(Q_DOWN + d, w2[bass.ds(i * 6 + d, 1)].rearrange("u p f n -> p (u f) n"), 2, i)
            embedding(0, Q_PROJ)
            load(Q_K, A["w_k"].rearrange("(k p) n -> p k n", p=P), KC)
            load(Q_V, A["w_v"].rearrange("(k p) n -> p k n", p=P), KC)
            sp.wait_ge(pl_ready, 1)
            sp.dma_start(pT[:, :].rearrange("p (k t) -> p k t", k=2), A["pT"][1].rearrange("(k p) t -> p k t", p=P)).then_inc(p_loaded, 16)
            for w, q in (("w_q", Q_Q), ("w_o", Q_O)):
                for u in range(4):
                    load(q + u, columns(A[w], u), KC)
            sp.wait_ge(k_ready, 2)
            sp.wait_ge(v_ready, 2)
            sp.wait_ge(cache_loaded, 32)
            sp.dma_start(A["kT_prompt"].rearrange("(a p) t -> p a t", p=P), kTt[:, :, TP - 128:TP]).then_inc(kv_stored, 16)
            sp.dma_start(A["kT_sample"].rearrange("(a p) t -> p a t", p=P), kTt[:, :, TP + 64:TP + 192]).then_inc(kv_stored, 16)
            sp.dma_start(A["v_prompt"], vv[:, 1, :]).then_inc(kv_stored, 16)
            sp.dma_start(A["v_sample"][0:64], vv[64:128, 3, :]).then_inc(kv_stored, 16)
            sp.dma_start(A["v_sample"][64:128], vv[0:64, 2, :]).then_inc(kv_stored, 16)
            for n in range(NRAW):
                expert(0, n)
            sp.wait_ge(routed, 1)
            m = sp.value_load(extra[0:1, 0:1], min_val=0, max_val=2)
            with sp.Fori(0, m * NE + (NE - 1)) as i:
                for n in range(NRAW, NU):
                    expert(i % NE, n, i * RND)
                for n in range(NRAW):
                    kind, b = SEQ[n // 2]
                    w, h = A["w1_moe" if kind == "g" else "w3_moe"], n % 2
                    load(Q_MOE + NU + n, w[bass.ds((i + 1) % NE, 1), 512 * h:512 * h + 512, 512 * b:512 * b + 512]
                         .rearrange("a (k p) n -> p (a k) n", p=P), 4, i * RND)
            last = m * (NE * RND) + (NE - 1) * RND
            for n in range(NRAW, NU):
                expert(NE - 1, n, last)
            embedding(1, Q_MOE + NU, last)
            yo = A["yT"].rearrange("(k p) t -> p k t", p=P)
            for c in range(0, KC, 2):
                sp.wait_ge(h_ready, 7 * KC + c + 2)
                sp.dma_start(yo[:, c:c + 2, :], hT[:, c:c + 2, :]).then_inc(y_stored, 16)
            sp.wait_ge(pool_stored, 32)
            sp.wait_ge(kv_stored, 80)
            sp.wait_ge(y_stored, 64)

        NCONST = 16

        @block.gpsimd
        def _(pool):
            pool.memset(ones[:, :], 1.0).then_inc(consts, 1)
            pool.memset(eps[:, :], EPS).then_inc(consts, 1)
            pool.memset(hcat[:, :, 0:HIST], 0.0).then_inc(hzero, 1)
            pool.dma_start(hcat[:, :, PADS - HIST:PADS], A["histT"].rearrange("(k p) t -> p k t", p=P)).then_inc(hist_loaded, 16)
            pool.iota(iota_i[:, :], pattern=[[1, 16]], base=1, channel_multiplier=0).then_inc(consts, 1)
            pool.iota(iota[:, :], pattern=[[1, T]], base=0, channel_multiplier=0,
                      allow_small_or_imprecise_dtypes=True).then_inc(consts, 1)
            pool.iota(tg[:, :, 0], pattern=[[P, 3]], base=0, channel_multiplier=1,
                      allow_small_or_imprecise_dtypes=True).then_inc(consts, 1)
            pool.wait_ge(consts, 5)
            pool.affine_select(out=ident[:, :], in_=ones[:, :], compare_op=ALU.is_equal, fill=0.0, base=0,
                               pattern=[[-1, P]], channel_multiplier=1).then_inc(consts, 1)
            pool.affine_select(out=tri[:, :], in_=ones[:, :], compare_op=ALU.is_gt, fill=0.0, base=0,
                               pattern=[[1, P]], channel_multiplier=-1).then_inc(consts, 1)
            pool.memset(mask[:, :], 0.0).then_inc(consts, 1)
            pool.memset(valid[:, :, :], 1.0).then_inc(consts, 1)
            pool.memset(onesb[:, :], 1.0).then_inc(consts, 1)
            pool.wait_ge(consts, 10)
            pool.tensor_copy(identb[:, :], ident[:, :]).then_inc(consts, 1)
            pool.tensor_copy(trib[:, :], tri[:, :]).then_inc(consts, 1)
            pool.wait_ge(consts, 12)
            pool.memset(valid[TS:P, 2, :], 0.0).then_inc(consts, 1)
            pool.wait_ge(consts, 13)
            pool.memset(mask[0:64, 192:256], NEG).then_inc(consts, 1)
            pool.wait_ge(consts, 14)
            pool.memset(mask[64:128, 0:64], NEG).then_inc(consts, 1)
            pool.wait_ge(consts, 15)
            pool.memset(mask[0:64, 320:384], NEG).then_inc(consts, 1)
            for z in (lg[:, :, :], PT[:, :].bitcast(F32)):
                pool.memset(z, 0.0).then_inc(consts, 1)
            def lo(q):
                pool.wait_ge(hi_ready, q + 1)
                if q:
                    pool.wait_ge(lo_ready, q)
                nc.gpsimd.tensor_tensor(Sl[:, q % NSPL, :], raw[:, q % NRAW, :], Sh[:, q % NSPL, :].bitcast(F32),
                                        ALU.subtract).then_inc(lo_ready, 1)

            lo(0)
            pool.wait_ge(hcat_ready, 4)
            src, n = hcat, 1
            for step, dst in enumerate((sA, sB, sA, sB)):
                if step:
                    pool.wait_ge(sums_ready, step)
                nc.gpsimd.tensor_tensor(dst[:, 6:KC, 2 * n - 1:], src[:, 6:KC, 2 * n - 1:], src[:, 6:KC, n - 1:LCAT - n], ALU.add).then_inc(sums_ready, 1)
                src, n = dst, 2 * n

            lo(1)
            lo(2)
            pool.wait_ge(hcat_ready, 16)
            for name, a in (("poolT_prompt", PADP + TP - HIST), ("poolT_sample", PADS + TS - HIST)):
                pool.dma_start(A[name].rearrange("(k p) t -> p k t", p=P), hcat[:, :, a:a + HIST]).then_inc(pool_stored, 16)
            lo(Q_GATE + 1)
            pool.wait_ge(unit_done, Q_MOE)
            for z in (ysh, ysl):
                pool.memset(z.bitcast(F32), 0.0).then_inc(consts, 1)

        @block.scalar
        def _(act):
            act.dma_start(br[:, :], A["br"]).then_inc(small_loaded, 16)
            act.dma_start(sinks[:, :], A["sinks"]).then_inc(small_loaded, 16)
            act.dma_start(wr[:, :, :], A["w_router"].rearrange("(k p) n -> p k n", p=P)).then_inc(small_loaded, 16)
            act.dma_start(pT[:, :].rearrange("p (k t) -> p k t", k=2), A["pT"][0].rearrange("(k p) t -> p k t", p=P)).then_inc(p_loaded, 16)
            act.sem_inc(silu_done, 2)

            def hi(q, r=0):
                act.wait_ge(raw_loaded[q % NRAW], r * 16 + 16 * (q // NRAW + 1))
                if q >= NSPL:
                    act.wait_ge(unit_done, r * NRAW + (q - NSPL + 1))
                nc.scalar.activation(Sh[:, q % NSPL, :], raw[:, q % NRAW, :], ACT.Copy).then_inc(hi_ready, 1)

            tables = [0]

            def table(f):
                tables[0] += 1
                nc.scalar.activation(spare[:, tables[0]:tables[0] + 1], eps[:, :], f)

            def squares(k, c0, c1):
                for c in range(c0, c1):
                    act.wait_ge(x_ready, KC * (k - 1) + c + 1)
                    nc.scalar.activation(sq3[:, c, :], xT[:, c, :], ACT.Square).then_inc(sq_ready, 1)

            def root(k):
                act.wait_ge(stat_done, k + 1)
                nc.scalar.activation(std[:, :], PS[:, 7, 0:T], ACT.Sqrt, bias=eps[:, :], scale=1.0 / D).then_inc(std_ready, 1)

            def high_h(s, c0=0, c1=KC):
                for c in range(c0, c1):
                    act.wait_ge(h_ready, KC * (s + (s == 5)) + c + 1)
                    nc.scalar.activation(Ah3[:, c, :], hT[:, c, :], ACT.Copy).then_inc(hh_ready, 1)

            act.wait_ge(consts, 2)
            table(ACT.Sqrt)
            for c in range(KC):
                if c % 4 == 0:
                    act.wait_ge(x_loaded[c // 4], 16)
                nc.scalar.activation(sq3[:, c, :], xT[:, c, :], ACT.Square).then_inc(sq_ready, 1)
            hi(0)
            root(0)
            hi(1)
            hi(2)
            act.wait_ge(vec_loaded, 16)
            high_h(0)
            squares(1, 0, KC)
            root(1)
            high_h(1)
            hi(3)

            def silu(r, b):
                act.wait_ge(unit_done, r * 6 + (Q_UP + 2 * b + 1))
                act.wait_ge(gu_ready, r * 6 + (2 * b + 2))
                for f in range(2):
                    nc.scalar.activation(sg[:, f, :], PS[:, f, 0:T], ACT.Silu).then_inc(silu_done, 1)

            def high_gu(d, src):
                o = GUOFF[d % 3]
                nc.scalar.activation(view(Ah, o, 2 * T), src, ACT.Copy).then_inc(gh_ready, 1)

            with act.Fori(0, 4) as i:
                for j in range(6):
                    if j % 2 == 0:
                        silu(i, j // 2)
                    hi(Q_UP + j + NSPL, i)
            silu(0, 12)
            hi(28)
            hi(29)
            high_gu(0, G[:, 0:2 * T])
            silu(0, 13)
            hi(30)
            act.wait_ge(gu_ready, 2 * NUP + 2)
            act.wait_ge(unit_done, Q_DOWN)
            high_gu(1, G[:, 2 * T:4 * T])
            with act.Fori(0, 2) as i:
                for d in range(2, 8):
                    act.wait_ge(unit_done, i * 6 + (Q_DOWN + d - 2))
                    high_gu(d, G[:, bass.ds(i * (12 * T) + 2 * T * d, 2 * T)])
                    hi(Q_DOWN + d, i)

            hi(Q_PROJ)
            hi(Q_PROJ + 1)
            table(ACT.Sqrt)
            act.wait_ge(p_loaded, 16)
            nc.scalar.activation(view(Ah, PA[0], 2 * T), pT[:, :], ACT.Copy).then_inc(ph_ready, 1)

            def gate_phase(layer, k, s, q, r, ahead):
                def embedding(n):
                    if n < KC - 1:
                        act.wait_ge(part_done, 7 * (15 + layer) + n + 1)
                    else:
                        act.wait_ge(unit_done, r * NRAW + (q + 1))
                    nc.scalar.activation(ep3[:, ORD[n], :], PS[:, ORD[n], 0:T], ACT.Copy).then_inc(eple_ready, 1)

                if layer:
                    for n in range(4):
                        embedding(n)
                squares(k, 0, KC)
                if ahead:
                    hi(q + 2, r)
                root(k)
                for c in range(KC):
                    high_h(s, c, c + 1)
                    if c >= 4 * layer:
                        embedding(c)
                hi(q + 3, r)
                for u in range(4):
                    for c in (2 * u, 2 * u + 1):
                        if c % 2:
                            act.wait_ge(unit_done, r * NRAW + (q + 2 + u))
                        else:
                            act.wait_ge(half_done, 12 * layer + u + 1)
                        if c >= 2:
                            act.wait_ge(x_ready, KC * k + c - 1)
                        nc.scalar.activation(sig[:, c % 2, :], PS[:, c, 0:T], ACT.Sigmoid).then_inc(sig_ready, 1)
                    if u == 3:
                        table(ACT.Sqrt)
                    if u:
                        squares(k + 1, 2 * u - 2, 2 * u)
                    if u < 3 and (ahead or u == 0):
                        hi(q + 4 + u, r)
                squares(k + 1, KC - 2, KC)
                root(k + 1)

            gate_phase(0, 2, 2, Q_PROJ, 0, True)
            high_h(3)
            hi(Q_GATE + 6)
            high_h(4)
            act.dma_start(kTt[:, :, TP:TP + 128], A["cache_kT"].rearrange("(a p) t -> p a t", p=P)).then_inc(cache_loaded, 16)
            act.dma_start(vv[:, 3, :], A["cache_v"]).then_inc(cache_loaded, 16)
            hi(Q_K + 3)
            for a in range(2):
                nc.scalar.activation(kTt[:, a, 0:TP], PS[:, 4 + a, 0:TP], ACT.Identity, bias=vec[:, B_K, a:a + 1])
                nc.scalar.activation(kTt[:, a, TP + 128:NKEY], PS[:, 4 + a, TP:T], ACT.Identity,
                                     bias=vec[:, B_K, a:a + 1]).then_inc(k_ready, 1)
            for a in range(2):
                nc.scalar.activation(vT[:, a, :], PS[:, 6 + a, 0:T], ACT.Identity, bias=vec[:, B_V, a:a + 1]).then_inc(vT_ready, 1)
            hi(Q_V + 3)

            def query(u):
                for c in (2 * u, 2 * u + 1):
                    if c % 2:
                        act.wait_ge(unit_done, Q_Q + u + 1)
                    else:
                        act.wait_ge(half_done, 5 + u)
                    nc.scalar.activation(qT[:, c, :], PS[:, QBANK[u] + c % 2, 0:T], ACT.Identity, bias=vec[:, B_Q, c:c + 1]).then_inc(q_ready, 1)
                hi(Q_Q + u + 3)

            def exps(j):
                b0, o = 2 * (j % 2), 25 * (j % 2)
                neg, acc = st[:, o + 5:o + 10], st[:, o + 15:o + 20]
                act.wait_ge(max_ready, j + 1)
                if j >= 2:
                    act.wait_ge(pT_done, 2 * j - 2)
                for h in range(2):
                    nc.scalar.activation(pp[:, b0 + h, 0:256], PS[:, b0 + h, 0:256], ACT.Exp, scale=0.125,
                                         bias=neg[:, h:h + 1], accum_out=acc[:, h:h + 1])
                    nc.scalar.activation(pp[:, b0 + h, 256:384], PS[:, b0 + h, 256:384], ACT.Exp, scale=0.125,
                                         bias=neg[:, 2 + h:3 + h], accum_out=acc[:, 2 + h:3 + h])
                nc.scalar.activation(psm[:, j % 2, 0:192].rearrange("p (b n) -> p b n", b=2), PS[:, b0:b0 + 2, 384:480], ACT.Exp,
                                     scale=0.125, bias=neg[:, 4:5], accum_out=acc[:, 4:5])
                nc.scalar.activation(st[:, o + 20:o + 25], st[:, o + 10:o + 15], ACT.Exp).then_inc(exp_done, 1)

            def high_o(j):
                act.wait_ge(pv_done, j + 1)
                nc.scalar.activation(Ah3[:, j, :], PS[:, PVBANK[j % 2], 0:T], ACT.Copy).then_inc(oh_ready, 1)

            table(ACT.Exp)
            query(0)
            query(1)
            query(2)
            exps(0)
            exps(1)
            query(3)
            for j in range(KC):
                if j >= 2:
                    high_o(j - 2)
                if 1 <= j < KC - 1:
                    exps(j + 1)
                for n in range(2):
                    act.wait_ge(pT_done, 2 * j + n + 1)
                    nc.scalar.activation(pTr[:, 2 * (j % 2) + n, :], PS[:, 5 + n, :], ACT.Copy).then_inc(pT_ready, 1)
            high_o(KC - 2)
            high_o(KC - 1)
            table(ACT.Sqrt)
            hi(Q_O + 3)
            for u in range(4):
                squares(4, 2 * u, 2 * u + 2)
                if u < 2:
                    hi(Q_O + u + 4)
            root(4)
            table(ACT.Exp)
            act.wait_ge(small_loaded, 48)
            act.wait_ge(lgT_done, 1)
            nc.scalar.activation(lgT[:, :], PS[0:NE, 0, 0:T], ACT.Identity, bias=br[:, :]).then_inc(lgT_ready, 1)
            act.wait_ge(top_ready, 1)
            nc.scalar.activation(rt[:, :, 1], rt[:, :, 0], ACT.Exp).then_inc(gexp_ready, 1)
            table(ACT.Silu)
            for n in range(6):
                act.wait_ge(hrow_done, n + 1)
                t, half = n // 2, n % 2
                r = TS if t == 2 else P
                nc.scalar.activation(hrow[0:r, t, 512 * half:512 * half + 512], PS[0:r, 2 + n % 4, :], ACT.Copy).then_inc(hrow_ready, 1)

            def high_x(hf, count):
                act.wait_ge(gath_done, count)
                nc.scalar.activation(view(Ah, 512 * hf, 512), PS[:, 1 + 3 * hf, :], ACT.Copy).then_inc(xh_ready, 1)

            hi(Q_O + 6)
            high_x(0, 1)
            high_x(1, 2)
            act.wait_ge(p_loaded, 32)
            nc.scalar.activation(view(Ah, PA[1], 2 * T), pT[:, :], ACT.Copy).then_inc(ph_ready, 1)
            act.wait_ge(routed, 1)
            m = act.value_load(extra[0:1, 0:1], min_val=0, max_val=2)
            with act.Fori(0, m * NE + NE) as i:
                def high_t(b):
                    act.wait_ge(t_done, i * NBK + (b + 1))
                    nc.scalar.activation(view(Ah, 1024 + 512 * (b % 2), 512), PS[:, 0, :], ACT.Copy).then_inc(th_ready, 1)

                for n in range(NU):
                    kind, b = SEQ[n // 2]
                    if n % 2 and kind == "g":
                        act.wait_ge(unit_done, i * NU + (Q_MOE + n + 1))
                        nc.scalar.activation(sgm[:, b % 2, :], PS[:, 2 + 2 * (b % 2), :], ACT.Silu).then_inc(msilu_done, 1)
                    if n % 2 == 0 and kind == "u" and b:
                        high_t(b - 1)
                    if n == NU - 3:
                        high_t(NBK - 1)
                        high_x(0, i * 2 + 3)
                        high_x(1, i * 2 + 4)
                    if n == NU - 1:
                        act.wait_ge(unit_done, i * NU + (Q_MOE + NU))
                        for hf in range(2):
                            nc.scalar.activation(ysh[:, 512 * hf:512 * hf + 512], PS[:, 6 + hf, :], ACT.Copy,
                                                 scale=si[:, 1:2]).then_inc(yh_ready, 1)
                    hi(Q_MOE + n + NSPL, i * RND)
            end = m * (NE * RND) + (NE - 1) * RND
            table(ACT.Sqrt)
            gate_phase(1, 5, 5, Q_MOE + NU, end, False)

        @block.tensor
        def _(pe):
            def mm(out, w, m, start, stop, **kw):
                return nc.tensor.matmul(out, w, m, start=start, stop=stop, **kw)

            def mm3(out, wh, wl, xh, xl, start, stop, **kw):
                mm(out, wh, xh, start, False, **kw)
                mm(out, wh, xl, False, False, **kw)
                return mm(out, wl, xh, False, stop, **kw)

            def unit(q, k, r=0):
                pe.wait_ge(lo_ready, r * NRAW + (q + 1))
                return (s[:, q % NSPL, :].rearrange("p (k n) -> p k n", k=k) for s in (Sh, Sl))

            def dense(out, wh, wl, c, xh, xl, ready=None):
                for k in range(KC):
                    if ready:
                        pe.wait_ge(ready[0], ready[1] + k + 1)
                    last = mm3(out, wh[:, k, P * c:P * c + P], wl[:, k, P * c:P * c + P], xh[:, k, :], xl[:, k, :], k == 0, k == KC - 1)
                return last

            pe.wait_ge(consts, NCONST)

            def norm(k):
                for c in range(KC):
                    pe.wait_ge(sq_ready, KC * k + c + 1)
                    last = mm(PS[:, 7, 0:T], ones[:, :], sq3[:, c, :], c == 0, c == KC - 1)
                last.then_inc(stat_done, 1)

            norm(0)
            wh, wl = unit(Q_POOL, KC)
            for c in range(KC):
                g, o = c // 2, P * (c % 2)
                pe.wait_ge(hl_ready, 2 * g + 2)
                for i in (2 * g, 2 * g + 1):
                    last = mm3(PS[:, 7 - c, 0:T], wh[:, i, o:o + P], wl[:, i, o:o + P], Ah3[:, i, :], Al3[:, i, :], i == 2 * g, i == 2 * g + 1)
                last.then_inc(unit_done if c == KC - 1 else part_done, 1)
            pe.wait_ge(x_ready, 1)
            norm(1)

            def up_unit(j, r=0):
                wh, wl = unit(Q_UP + j, KC, r)
                b = j // 2
                if j % 2 == 0:
                    pe.wait_ge(silu_done, r * 6 + (2 * b + 2))
                else:
                    pe.wait_ge(gu_ready, r * 6 + (2 * b + 2))
                for f in range(2):
                    last = dense(PS[:, 2 * (j % 2) + f, 0:T], wh, wl, f, Ah3, Al3)
                last.then_inc(unit_done, 1)

            def chunk_by_chunk(q, banks, s, left=None):
                w = [tuple(unit(q + n, KC)) for n in range(len(banks))]
                for k in range(KC):
                    pe.wait_ge(hl_ready, KC * s + k + 1)
                    for (wh, wl), bank in zip(w, banks):
                        for f in range(2):
                            last = mm3(PS[:, bank + f, 0:T], wh[:, k, P * f:P * f + P], wl[:, k, P * f:P * f + P], Ah3[:, k, :], Al3[:, k, :],
                                       k == 0, k == KC - 1, skip_group_check=True)
                    if left is not None and k < KC - 1:
                        last.then_inc(left, 1)
                last.then_inc(unit_done, len(banks))

            chunk_by_chunk(Q_UP, (0, 2), 1)
            for j in range(2, 6):
                up_unit(j)
            with pe.Fori(1, 4) as i:
                for j in range(6):
                    up_unit(j, i)
            for j in range(24, 2 * NUP):
                up_unit(j)

            def down_unit(d, r=0):
                wh, wl = unit(Q_DOWN + d, 2, r)
                pe.wait_ge(gl_ready, r * 6 + (d + 1))
                o = GUOFF[d % 3]
                gh, gl = view(Ah, o, 2 * T, 2), view(Al, o, 2 * T, 2)
                for c in range(KC):
                    if d == 0 and c == 4:
                        pe.wait_ge(gu_ready, 2 * NUP + 2)
                    for f in range(2):
                        last = mm3(PS[:, 7 - c, 0:T], wh[:, f, P * c:P * c + P], wl[:, f, P * c:P * c + P], gh[:, f, :], gl[:, f, :],
                                   d == 0 and f == 0, True, skip_group_check=True)
                    last.then_inc(unit_done if c == KC - 1 else part_done, 1)

            down_unit(0)
            down_unit(1)
            with pe.Fori(0, 2) as i:
                for d in range(2, 8):
                    down_unit(d, i)

            def embed(layer, q, r, chunks):
                wh, wl = unit(q, 2, r)
                pe.wait_ge(pl_ready, layer + 1)
                pAh, pAl = (view(x, PA[layer], 2 * T, 2) for x in (Ah, Al))
                for c in chunks:
                    if c == KC - 1:
                        pe.wait_ge(std_ready, 3 * layer + 3)
                    for i in range(2):
                        last = mm3(PS[:, c, 0:T], wh[:, i, P * c:P * c + P], wl[:, i, P * c:P * c + P], pAh[:, i, :], pAl[:, i, :], i == 0, i == 1)
                    last.then_inc(unit_done if c == KC - 1 else part_done, 1)

            def gate_phase(layer, k, s, q, r):
                norm(k)
                embed(layer, q, r, ORD[4 * layer:])
                for u in range(4):
                    wh, wl = unit(q + 1 + u, KC, r)
                    for f in range(2):
                        pe.wait_ge(eple_ready, KC * layer + ORD.index(2 * u + f) + 1)
                        dense(PS[:, 2 * u + f, 0:T], wh, wl, f, Ah3, Al3, (hl_ready, KC * s)).then_inc(unit_done if f else half_done, 1)
                pe.wait_ge(sig_ready, KC * (layer + 1))
                norm(k + 1)

            gate_phase(0, 2, 2, Q_PROJ, 0)
            pe.wait_ge(std_ready, 4)
            chunk_by_chunk(Q_K, (4, 6), 3, kv_left)

            def scores(j):
                a, b0 = j // 4, 2 * (j % 2)
                for b in range(2):
                    bank, o = b0 + b, 64 * b
                    mm(PS[:, bank, 0:384], identb[:, :], mask[:, :], True, False, skip_group_check=True)
                    mm(PS[:, bank, 0:256], qT[o:o + 64, j, P:2 * P], kTt[o:o + 64, a, 0:TP], False, False, skip_group_check=True)
                    mm(PS[:, bank, 256:384], qT[o:o + 64, j, 0:P], kTt[o:o + 64, a, 0:P], False, True, skip_group_check=True)
                for b in range(2):
                    o = 64 * b
                    for half in range(2):
                        last = mm(PS[o:o + 64, b0 + half, 384:480], qT[o:o + 64, j, TP:T],
                                  kTt[o:o + 64, a, TP + 96 * half:TP + 96 * half + 96], True, True, skip_group_check=True)
                last.then_inc(score_done, 1)

            for u in range(4):
                if u == 3:
                    pe.wait_ge(cache_loaded, 32)
                    pe.wait_ge(q_ready, 2)
                    scores(0)
                    pe.wait_ge(q_ready, 4)
                    scores(1)
                    pe.wait_ge(v_ready, 3)
                if u == 2:
                    pe.wait_ge(vT_ready, 2)
                wh, wl = unit(Q_Q + u, KC)
                for f in range(2):
                    dense(PS[:, QBANK[u] + f, 0:T], wh, wl, f, Ah3, Al3, (hl_ready, 4 * KC)).then_inc(unit_done if f else half_done, 1)
                if u == 0:
                    pe.wait_ge(vT_ready, 2)
                    pe.wait_ge(k_ready, 2)
                    for t in range(3):
                        n = TS if t == 2 else P
                        for a in range(2):
                            o = 256 * (t % 2) + P * a
                            last = nc.tensor.transpose(PS[0:n, 4 + t // 2, o:o + P], vT[:, a, P * t:P * t + n], ident[:, :])
                    last.then_inc(vt_done, 1)
            pe.wait_ge(q_ready, KC)

            def transposed(j):
                for n in range(2):
                    pe.wait_ge(p_ready, 2 * j + n + 1)
                    if j:
                        pe.wait_ge(pT_ready, 2 * j + n - 1)
                    for blk in range(4):
                        src = psm[:, j % 2, P * n:P * n + P] if blk == 3 else pp[:, 2 * (j % 2) + n, P * blk:P * blk + P]
                        last = nc.tensor.transpose(PS[:, 5 + n, P * blk:P * blk + P], src, ident[:, :])
                    last.then_inc(pT_done, 1)

            def outputs(j):
                a = j // 4
                pe.wait_ge(pT_ready, 2 * j + 2)
                if j >= 2:
                    pe.wait_ge(ol_ready, j - 1)
                for b in range(2):
                    o, h, bank = 64 * b, 2 * (j % 2) + b, PVBANK[j % 2]
                    vc = 64 * (2 * a + b)
                    mm(PS[o:o + 64, bank, P:2 * P], vv[:, 0, vc:vc + 64], pTr[:, h, 0:P], True, False)
                    mm(PS[o:o + 64, bank, P:2 * P], vv[:, 1, vc:vc + 64], pTr[:, h, P:2 * P], False, True)
                    mm(PS[o:o + 64, bank, 0:P], vv[:, 0, vc:vc + 64], pTr[:, h, 2 * P:3 * P], True, True)
                    mm(PS[o:o + 64, bank, TP:T], vv[:, 3, vc:vc + 64], pTr[:, 2 * (j % 2), 384 + o:384 + o + 64], True, False)
                    last = mm(PS[o:o + 64, bank, TP:T], vv[0:64, 2, vc:vc + 64], pTr[0:64, 2 * (j % 2) + 1, 384 + o:384 + o + 64], False, True)
                last.then_inc(pv_done, 1)

            for j in range(KC):
                transposed(j)
                if j < KC - 2:
                    pe.wait_ge(exp_done, j + 1)
                    scores(j + 2)
                if j:
                    outputs(j - 1)
            outputs(KC - 1)
            for u in range(4):
                wh, wl = unit(Q_O + u, KC)
                if u >= 2:
                    pe.wait_ge(x_ready, 3 * KC + 2 * u - 2)
                for f in range(2):
                    dense(PS[:, 2 * (u % 2) + f, 0:T], wh, wl, f, Ah3, Al3, (ol_ready, 0)).then_inc(unit_done if f else half_done, 1)
            norm(4)
            pe.wait_ge(small_loaded, 48)
            for k in range(KC):
                pe.wait_ge(h_ready, 5 * KC + k + 1)
                last = mm(PS[0:NE, 0, 0:T], wr[:, k, :], hT[:, k, :], k == 0, k == KC - 1)
            last.then_inc(lgT_done, 1)

            def rows(n):
                t, half = n // 2, n % 2
                r = TS if t == 2 else P
                if n >= 4:
                    pe.wait_ge(hrow_ready, n - 3)
                for q in range(4):
                    last = nc.tensor.transpose(PS[0:r, 2 + n % 4, P * q:P * q + P], hT[:, 4 * half + q, P * t:P * t + r], ident[:, :])
                last.then_inc(hrow_done, 1)

            rows(0)
            pe.wait_ge(lgT_ready, 1)
            for t in range(3):
                n = TS if t == 2 else P
                last = nc.tensor.transpose(PS[0:n, 1, NE * t:NE * t + NE], lgT[:, P * t:P * t + n], ident[0:NE, 0:NE])
            last.then_inc(lg_done, 1)
            rows(1)
            rows(2)
            pe.wait_ge(sel_ready, 1)
            for t in range(4):
                for i in range(min(t, 2) + 1):
                    w = trib if i == t else onesb
                    last = mm(PS[:, 1, 8 * t:8 * t + 8], w[:, :], sel[:, i, :], i == 0, i == min(t, 2))
            last.then_inc(pos_done, 1)
            for n in range(3, 6):
                rows(n)
            pe.wait_ge(hrow_ready, 6)

            def gather(hf):
                for c in range(4):
                    for t in range(3):
                        r = TS if t == 2 else P
                        last = mm(PS[:, 1 + 3 * hf, P * c:P * c + P], hrow[0:r, t, 512 * hf + P * c:512 * hf + P * c + P], Pm[0:r, t, :],
                                  t == 0, t == 2)
                last.then_inc(gath_done, 1)

            def slot_info():
                for t in range(3):
                    last = mm(PS[:, 5, 0:2], Pm[:, t, :], tg[:, t, :], t == 0, t == 2)
                last.then_inc(slots_done, 1)

            pe.wait_ge(P_ready, 1)
            gather(0)
            gather(1)
            slot_info()

            def scatter(c, bank=1):
                mm(PS[:, bank, 0:T], ysh[:, P * c:P * c + P], PT[:, :], True, False)
                mm(PS[:, bank, 0:T], ysl[:, P * c:P * c + P], PT[:, :], False, True).then_inc(scat_done, 1)

            pe.wait_ge(routed, 1)
            m = pe.value_load(extra[0:1, 0:1], min_val=0, max_val=2)
            with pe.Fori(0, m * NE + NE) as i:
                def scatter_next(c):
                    if c == 0:
                        pe.wait_ge(yl_ready, i * 2 + 2)
                        pe.wait_ge(PT_ready, i + 1)
                    else:
                        pe.wait_ge(y_added, i * KC + c)
                    scatter(c)

                def up(kind, b, h):
                    n = POS[kind, b] + h
                    bank = 2 + 2 * (b % 2) + (kind == "u")
                    if kind == "g" and b == 0:
                        pe.wait_ge(xl_ready, i * 2 + (h + 1))
                    if kind == "u" and b == 1 and h == 0:
                        pe.wait_ge(si_ready, i + 1)
                    if kind == "g" and b != 1 and h == 0:
                        pe.wait_ge(gum_ready, i * NBK + (b + 1 if b == 0 else b))
                    wh, wl = unit(Q_MOE + n, 4, i * RND)
                    for k in range(4):
                        if 1 <= n < KC and k == 3:
                            scatter_next(n - 1)
                        last = mm3(PS[:, bank, :], xgh[:, 4 * h + k, :], xgl[:, 4 * h + k, :], wh[:, k, :], wl[:, k, :],
                                   h == 0 and k == 0, h == 1 and k == 3)
                    last.then_inc(unit_done, 1)

                def transposes(b):
                    pe.wait_ge(gum_ready, i * NBK + (b + 2))
                    pe.wait_ge(tl_ready, i * NBK + (b + 1))
                    for q in range(4):
                        last = nc.tensor.transpose(PS[:, 0, P * q:P * q + P], gum[:, b % 2, P * q:P * q + P], ident[:, :])
                    last.then_inc(t_done, 1)

                def down(b, h):
                    if h == 0:
                        pe.wait_ge(tl_ready, i * NBK + (b + 2))
                    wh, wl = unit(Q_MOE + POS["d", b] + h, 2, i * RND)
                    for f in range(2):
                        if (b, h, f) == (0, 0, 1):
                            scatter_next(KC - 1)
                        for hf in range(2):
                            j = 4 * (b % 2) + 2 * h + f
                            last = mm3(PS[:, 6 + hf, :], gth[:, j, :], gtl[:, j, :], wh[:, f, 512 * hf:512 * hf + 512], wl[:, f, 512 * hf:512 * hf + 512],
                                       b == 0 and h == 0 and f == 0, b == NBK - 1 and h == 1 and f == 1)
                    last.then_inc(unit_done, 1)

                for kind, b in SEQ:
                    if kind == "u" and b:
                        transposes(b - 1)
                    if (kind, b) == ("d", NBK - 1):
                        transposes(NBK - 1)
                        pe.wait_ge(P_ready, i + 2)
                        gather(0)
                        gather(1)
                        slot_info()
                    for h in range(2):
                        if kind == "d":
                            down(b, h)
                        else:
                            up(kind, b, h)
            end = m * (NE * RND) + (NE - 1) * RND
            pe.wait_ge(xl_ready, m * (2 * NE) + (2 * NE + 2))
            embed(1, Q_MOE + NU, end, ORD[:4])
            pe.wait_ge(PT_ready, m * NE + (NE + 1))
            for c in range(KC):
                if c % 4 == 0:
                    pe.wait_ge(yl_ready, m * (2 * NE) + (2 * NE + 1 + c // 4))
                if c == 1:
                    pe.wait_ge(si_ready, m * NE + (NE + 1))
                if c >= 2:
                    pe.wait_ge(y_added, m * (NE * KC) + (NE * KC + c - 1))
                scatter(c, 5 if c % 2 else 1)
            pe.wait_ge(y_added, m * (NE * KC) + (NE * KC + KC))
            gate_phase(1, 5, 5, Q_MOE + NU, end)

        @block.vector
        def _(v):
            links = [0]

            def link(ins):
                links[0] += 1
                ins.then_inc(chain, 1)
                v.wait_ge(chain, links[0])

            def lo(q, r=0):
                v.wait_ge(hi_ready, r * NRAW + (q + 1))
                nc.vector.tensor_tensor(Sl[:, q % NSPL, :], raw[:, q % NRAW, :], Sh[:, q % NSPL, :].bitcast(F32),
                                        ALU.subtract).then_inc(lo_ready, 1)

            def low(out, x, high, done):
                return nc.vector.tensor_tensor(out, x, high.bitcast(F32), ALU.subtract).then_inc(done, 1)

            def norm(k):
                v.wait_ge(std_ready, k + 1)
                link(nc.vector.reciprocal(rstd[:, :], std[:, :]))

            def low_h(s, c):
                v.wait_ge(hh_ready, KC * s + c + 1)
                low(Al3[:, c, :], hT[:, c, :], Ah3[:, c, :], hl_ready)

            def scaled(g, s=None, left=False):
                for c in range(KC):
                    if left and c < KC - 1:
                        v.wait_ge(kv_left, c + 1)
                    elif left:
                        v.wait_ge(unit_done, Q_V + 1)
                    nc.vector.scalar_tensor_tensor(out=hT[:, c, :], in0=xT[:, c, :], scalar=vec[:, g, c:c + 1], in1=rstd[:, :],
                                                   op0=ALU.mult, op1=ALU.mult).then_inc(h_ready, 1)
                    if s is not None and c:
                        low_h(s, c - 1)
                if s is not None:
                    low_h(s, KC - 1)

            v.sem_inc(gu_ready, 2)
            v.sem_inc(tl_ready, 1)
            v.sem_inc(gum_ready, 1)
            v.sem_inc(PT_ready, 1)
            v.sem_inc(yl_ready, 2)
            v.wait_ge(consts, NCONST)
            link(nc.vector.tensor_copy(st[:, 0:16], iota_i[:, :]))
            link(nc.vector.reciprocal(inv[:, :], st[:, 0:16]))
            v.wait_ge(vec_loaded, 16)
            norm(0)
            v.wait_ge(hzero, 1)
            v.wait_ge(hist_loaded, 16)

            def normed(g):
                for c in (2 * g, 2 * g + 1):
                    for a, b, o in ((0, TP, PADP), (TP, T, PADS)):
                        nc.vector.scalar_tensor_tensor(out=hcat[:, c, o:o + b - a], in0=xT[:, c, a:b], scalar=vec[:, G_MIX0, c:c + 1],
                                                       in1=rstd[:, a:b], op0=ALU.mult, op1=ALU.mult).then_inc(hcat_ready, 1)

            normed(3)
            normed(0)
            for g, w in enumerate((2, 4, 8, 16)):
                k = slice(2 * g, 2 * g + 2)
                if g == 3:
                    v.wait_ge(sums_ready, 4)
                    src = sB
                else:
                    v.wait_ge(hcat_ready, 4 * g + 8)
                    src, n = hcat, 1
                    for dst in (sA, sB, sA)[0:g + 1]:
                        link(nc.vector.tensor_tensor(dst[:, k, 2 * n - 1:], src[:, k, 2 * n - 1:], src[:, k, n - 1:LCAT - n], ALU.add))
                        src, n = dst, 2 * n
                link(nc.vector.tensor_tensor(src[:, k, PADP:PADP + w - 1], src[:, k, PADP:PADP + w - 1],
                                             inv[:, None, 0:w - 1].broadcast_to([P, 2, w - 1]), ALU.mult))
                nc.vector.tensor_tensor(hT[:, k, 0:w - 1], src[:, k, PADP:PADP + w - 1], hcat[:, k, PADP:PADP + w - 1], ALU.subtract)
                for o, a, n in ((PADP + w - 1, w - 1, TP - w + 1), (PADS, TP, TS)):
                    last = nc.vector.scalar_tensor_tensor(out=hT[:, k, a:a + n], in0=src[:, k, o:o + n], scalar=1.0 / w, in1=hcat[:, k, o:o + n],
                                                          op0=ALU.mult, op1=ALU.subtract)
                last.then_inc(h_ready, 2)
                if g < 2:
                    normed(g + 1)
                low_h(0, 2 * g)
                low_h(0, 2 * g + 1)
            for c in range(KC):
                if c < KC - 1:
                    v.wait_ge(part_done, c + 1)
                else:
                    v.wait_ge(unit_done, Q_POOL + 1)
                nc.vector.scalar_tensor_tensor(out=xT[:, c, :], in0=PS[:, 7 - c, 0:T], scalar=vec[:, POOL_SC, c:c + 1],
                                               in1=xT[:, c, :], op0=ALU.mult, op1=ALU.add).then_inc(x_ready, 1)
            norm(1)
            scaled(G_FFN0, 1)
            v.wait_ge(lo_ready, 3)
            lo(3)
            v.wait_ge(pool_stored, 32)

            def glu_dense(r, b, out):
                v.wait_ge(silu_done, r * 6 + (2 * b + 4))
                v.wait_ge(unit_done, r * 6 + (Q_UP + 2 * b + 2))
                for f in range(2):
                    nc.vector.tensor_tensor(out(f), sg[:, f, :], PS[:, 2 + f, 0:T], ALU.mult).then_inc(gu_ready, 1)

            with v.Fori(0, 4) as i:
                for j in range(6):
                    if j % 2:
                        glu_dense(i, j // 2, lambda f: G[:, bass.ds(i * (6 * T) + (j // 2 * 2 + f) * T, T)])
                    lo(Q_UP + j + NSPL, i)

            def low_gu(d, src):
                low(view(Al, GUOFF[d % 3], 2 * T), src, view(Ah, GUOFF[d % 3], 2 * T), gl_ready)

            lo(28)
            glu_dense(0, 12, lambda f: guT[:, 24 + f, :])
            lo(29)
            v.wait_ge(gh_ready, 1)
            low_gu(0, G[:, 0:2 * T])
            lo(30)
            glu_dense(0, 13, lambda f: guT[:, 26 + f, :])
            v.wait_ge(gh_ready, 2)
            low_gu(1, G[:, 2 * T:4 * T])
            with v.Fori(0, 2) as i:
                for d in range(2, 8):
                    v.wait_ge(gh_ready, i * 6 + (d + 1))
                    low_gu(d, G[:, bass.ds(i * (12 * T) + 2 * T * d, 2 * T)])
                    lo(Q_DOWN + d, i)
            lo(Q_PROJ)
            lo(Q_PROJ + 1)
            v.wait_ge(ph_ready, 1)
            low(view(Al, PA[0], 2 * T), pT[:, :], view(Ah, PA[0], 2 * T), pl_ready)
            for c in range(KC):
                if c < KC - 1:
                    v.wait_ge(part_done, 7 * NUP + c + 1)
                else:
                    v.wait_ge(unit_done, Q_PROJ)
                nc.vector.tensor_tensor(xT[:, c, :], xT[:, c, :], PS[:, 7 - c, 0:T], ALU.add).then_inc(x_ready, 1)

            def gate_phase(layer, k, s, g, q, r, ahead):
                norm(k)
                scaled(g, s)
                if ahead:
                    v.wait_ge(lo_ready, q + 3)
                lo(q + 3, r)
                for c in range(KC):
                    v.wait_ge(eple_ready, KC * layer + ORD.index(c) + 1)
                    v.wait_ge(sig_ready, KC * layer + c + 1)
                    link(nc.vector.tensor_tensor(gtm[:, c % 2, :], sig[:, c % 2, :], ep3[:, c, :], ALU.mult))
                    nc.vector.tensor_tensor(xT[:, c, :], xT[:, c, :], gtm[:, c % 2, :], ALU.add).then_inc(x_ready, 1)
                    if c % 2 and c < KC - 1 and (ahead or c == 1):
                        lo(q + 4 + c // 2, r)

            gate_phase(0, 2, 2, G_PLE0, Q_PROJ, 0, True)
            norm(3)
            scaled(G_KV, 3)
            lo(Q_GATE + 6)
            scaled(G_MIX1, 4, True)
            lo(Q_K + 3)
            lo(Q_V + 3)
            v.wait_ge(vt_done, 1)
            nc.vector.tensor_copy(vv[:, 0:2, :], PS[:, 4, :].rearrange("p (t n) -> p t n", t=2)).then_inc(v_ready, 1)
            nc.vector.tensor_copy(vv[0:TS, 2, :], PS[0:TS, 5, 0:256]).then_inc(v_ready, 1)
            nc.vector.memset(psm[:, :, 192:256], 0.0).then_inc(v_ready, 1)
            for u in range(3):
                lo(Q_Q + u + 3)
            v.wait_ge(small_loaded, 48)

            def maxima(j):
                b0, o = 2 * (j % 2), 25 * (j % 2)
                mx, neg, ds_ = (st[:, o + 5 * i:o + 5 * i + 5] for i in range(3))
                v.wait_ge(score_done, j + 1)
                nc.vector.reduce_max(mx[:, 0:2], PS[:, b0:b0 + 2, 0:256], AX.X)
                nc.vector.reduce_max(mx[:, 2:4], PS[:, b0:b0 + 2, 256:384], AX.X)
                link(nc.vector.reduce_max(mx[:, 4:5], PS[:, b0:b0 + 2, 384:480], AX.XY))
                link(nc.vector.scalar_tensor_tensor(out=mx, in0=mx, scalar=0.125, in1=sinks[:, 5 * j:5 * j + 5], op0=ALU.mult, op1=ALU.max))
                nc.vector.tensor_scalar(neg, mx, -1.0, None, ALU.mult)
                nc.vector.tensor_tensor(ds_, sinks[:, 5 * j:5 * j + 5], mx, ALU.subtract).then_inc(max_ready, 1)

            def probabilities(j):
                b0, o = 2 * (j % 2), 25 * (j % 2)
                acc, es = st[:, o + 15:o + 20], st[:, o + 20:o + 25]
                v.wait_ge(exp_done, j + 1)
                link(nc.vector.tensor_tensor(acc, acc, es, ALU.add))
                link(nc.vector.reciprocal(acc, acc))
                nc.vector.tensor_scalar(psm[:, j % 2, 0:192], psm[:, j % 2, 0:192], acc[:, 4:5], None, ALU.mult)
                for h in range(2):
                    nc.vector.tensor_scalar(pp[:, b0 + h, 0:256], pp[:, b0 + h, 0:256], acc[:, h:h + 1], None, ALU.mult)
                    nc.vector.tensor_scalar(pp[:, b0 + h, 256:384], pp[:, b0 + h, 256:384], acc[:, 2 + h:3 + h], None, ALU.mult).then_inc(p_ready, 1)

            def low_o(j):
                v.wait_ge(oh_ready, j + 1)
                low(Al3[:, j, :], PS[:, PVBANK[j % 2], 0:T], Ah3[:, j, :], ol_ready)

            maxima(0)
            maxima(1)
            probabilities(0)
            probabilities(1)
            lo(Q_Q + 6)
            for j in range(1, KC + 2):
                if j < KC - 1:
                    maxima(j + 1)
                if j >= 2:
                    low_o(j - 2)
                if j < KC - 1:
                    probabilities(j + 1)
            lo(Q_O + 3)
            for u in range(4):
                for c in (2 * u, 2 * u + 1):
                    if c % 2:
                        v.wait_ge(unit_done, Q_O + u + 1)
                    else:
                        v.wait_ge(half_done, 9 + u)
                    nc.vector.tensor_tensor(xT[:, c, :], xT[:, c, :], PS[:, c % 4, 0:T], ALU.add).then_inc(x_ready, 1)
                if u < 2:
                    lo(Q_O + u + 4)
            norm(4)
            scaled(G_FFN1)
            v.wait_ge(consts, NCONST + 4)
            v.wait_ge(lg_done, 1)
            nc.vector.tensor_copy(lg[:, 0:2, :], PS[:, 1, 0:2 * NE].rearrange("p (t e) -> p t e", t=2))
            link(nc.vector.tensor_copy(lg[0:TS, 2, :], PS[0:TS, 1, 2 * NE:3 * NE]))
            for t in range(3):
                last = nc.vector.max(top[:, t, :], lg[:, t, :])
            link(last)
            for t in range(3):
                last = nc.vector.max_index(topi[:, t, :], top[:, t, :], lg[:, t, :])
            link(last)
            nc.vector.tensor_tensor(rt[:, :, 0], top[:, :, 1], top[:, :, 0], ALU.subtract).then_inc(top_ready, 1)
            link(nc.vector.tensor_copy(rt[:, :, 2:4], topi[:, :, 0:2]))
            numbers = iota[:, None, 0:NE].broadcast_to([P, 3, NE])

            def column(c):
                return rt[:, :, c:c + 1].broadcast_to([P, 3, NE])

            nc.vector.tensor_tensor(gate[:, :, :], numbers, column(2), ALU.is_equal)
            link(nc.vector.tensor_tensor(oh[:, :, :], numbers, column(3), ALU.is_equal))
            link(nc.vector.tensor_tensor(eq[:, :, :], gate[:, :, :], oh[:, :, :], ALU.add))
            nc.vector.tensor_tensor(sel[:, :, :], eq[:, :, :], valid[:, :, :], ALU.mult).then_inc(sel_ready, 1)
            v.wait_ge(gexp_ready, 1)
            link(nc.vector.tensor_scalar(rt[:, :, 0], rt[:, :, 1], 1.0, None, ALU.add))
            link(nc.vector.reciprocal(rt[:, :, 0], rt[:, :, 0]))
            link(nc.vector.tensor_tensor(rt[:, :, 1], rt[:, :, 1], rt[:, :, 0], ALU.mult))
            nc.vector.tensor_tensor(gate[:, :, :], gate[:, :, :], column(0), ALU.mult)
            link(nc.vector.tensor_tensor(oh[:, :, :], oh[:, :, :], column(1), ALU.mult))
            link(nc.vector.tensor_tensor(gate[:, :, :], gate[:, :, :], oh[:, :, :], ALU.add))
            v.wait_ge(pos_done, 1)
            link(nc.vector.scalar_tensor_tensor(out=posm[:, :, :], in0=PS[:, 1, 0:24].rearrange("p (t e) -> p t e", t=3), scalar=1.0,
                                                in1=sel[:, :, :], op0=ALU.add, op1=ALU.mult))
            nc.vector.tensor_scalar(posm[:, :, :], posm[:, :, :], -1.0, None, ALU.add).then_inc(stepped, 1)
            link(nc.vector.reduce_max(cnt[0:1, 0:1], PS[0:1, 1, 24:32], AX.X))
            nc.vector.tensor_scalar(cnt[0:1, 1:2], cnt[0:1, 0:1], float(P), None, ALU.is_gt)
            link(nc.vector.tensor_scalar(cnt[0:1, 2:3], cnt[0:1, 0:1], float(2 * P), None, ALU.is_gt))
            link(nc.vector.tensor_tensor(cnt[0:1, 3:4], cnt[0:1, 1:2], cnt[0:1, 2:3], ALU.add))
            nc.vector.tensor_copy(extra[0:1, 0:1], cnt[0:1, 3:4]).then_inc(routed, 1)

            def one_hots(e, steps):
                v.wait_ge(stepped, steps)
                for t in range(3):
                    nc.vector.tensor_scalar(Pm[:, t, :], iota[:, 0:P], posm[:, t, bass.ds(e, 1)], None, ALU.is_equal)
                nc.vector.tensor_copy(tg[:, :, 1:2], gate[:, :, bass.ds(e, 1)]).then_inc(P_ready, 1)
                v.wait_ge(P_ready, steps)
                nc.vector.tensor_scalar(posm[:, :, bass.ds(e, 1)], posm[:, :, bass.ds(e, 1)], float(-P), None, ALU.add).then_inc(stepped, 1)

            def low_x(hf, count):
                v.wait_ge(xh_ready, count)
                low(view(Al, 512 * hf, 512), PS[:, 1 + 3 * hf, :], view(Ah, 512 * hf, 512), xl_ready)

            def take_slots(count):
                v.wait_ge(slots_done, count)
                nc.vector.tensor_copy(si[:, :], PS[:, 5, 0:2]).then_inc(si_ready, 1)

            one_hots(0, 1)
            lo(Q_O + 6)
            low_x(0, 1)
            low_x(1, 2)
            take_slots(1)
            v.wait_ge(ph_ready, 2)
            low(view(Al, PA[1], 2 * T), pT[:, :], view(Ah, PA[1], 2 * T), pl_ready)
            v.wait_ge(routed, 1)
            m = v.value_load(extra[0:1, 0:1], min_val=0, max_val=2)

            def add_back(c, count, bank=1):
                v.wait_ge(scat_done, count)
                nc.vector.tensor_tensor(xT[:, c, :], xT[:, c, :], PS[:, bank, 0:T], ALU.add).then_inc(y_added, 1)

            with v.Fori(0, m * NE + NE) as i:
                def low_t(b):
                    v.wait_ge(th_ready, i * NBK + (b + 1))
                    o = 1024 + 512 * (b % 2)
                    low(view(Al, o, 512), PS[:, 0, :], view(Ah, o, 512), tl_ready)

                for n in range(NU):
                    kind, b = SEQ[n // 2]
                    if 1 <= n <= KC:
                        add_back(n - 1, i * KC + n)
                    if n == KC + 1:
                        v.wait_ge(si_ready, i + 1)
                        nc.vector.tensor_scalar(PT[:, :], iota[:, :], si[:, 0:1], None, ALU.is_equal).then_inc(PT_ready, 1)
                    if n % 2 and kind == "u":
                        v.wait_ge(msilu_done, i * NBK + (b + 1))
                        v.wait_ge(unit_done, i * NU + (Q_MOE + n + 1))
                        nc.vector.tensor_tensor(gum[:, b % 2, :], sgm[:, b % 2, :], PS[:, 3 + 2 * (b % 2), :], ALU.mult).then_inc(gum_ready, 1)
                    if n % 2 == 0 and kind == "u" and b:
                        low_t(b - 1)
                    if n == NU // 2:
                        one_hots((i + 1) % NE, i + 2)
                    if n == NU - 3:
                        low_t(NBK - 1)
                        low_x(0, i * 2 + 3)
                        low_x(1, i * 2 + 4)
                    if n == NU - 1:
                        for hf in range(2):
                            v.wait_ge(yh_ready, i * 2 + (hf + 1))
                            nc.vector.scalar_tensor_tensor(out=ysl[:, 512 * hf:512 * hf + 512], in0=PS[:, 6 + hf, :], scalar=si[:, 1:2],
                                                           in1=ysh[:, 512 * hf:512 * hf + 512].bitcast(F32), op0=ALU.mult,
                                                           op1=ALU.subtract).then_inc(yl_ready, 1)
                        v.wait_ge(yl_ready, i * 2 + 4)
                        take_slots(i + 2)
                    lo(Q_MOE + n + NSPL, i * RND)
            for c in range(KC + 1):
                if c < KC:
                    add_back(c, m * (NE * KC) + (NE * KC + c + 1), 5 if c % 2 else 1)
                if c:
                    v.wait_ge(y_added, m * (NE * KC) + (NE * KC + c))
                    v.sem_inc(x_ready, 1)
            gate_phase(1, 5, 5, G_PLE1, Q_MOE + NU, m * (NE * RND) + (NE - 1) * RND, False)
            norm(6)
            scaled(G_FIN)


def kernel(**inputs):
    import numpy as np
    import concourse.bacc as bacc
    from concourse.bass_utils import run_bass_kernel_spmd as run

    a = {k: np.asarray(x) for k, x in inputs.items()}

    def chunks(x):
        return x.reshape(KC, P).T

    heads = [(2 * aa + b) * 4 + r for aa in range(2) for r in range(4) for b in range(2)]
    bq = a["b_q"][0].reshape(16, 64)[heads].reshape(KC, P).T
    bk = np.zeros((P, KC), a["b_k"].dtype)
    bk[:, 0:2] = a["b_k"].reshape(2, P).T
    bv = np.zeros((P, KC), a["b_v"].dtype)
    bv[:, 0:2] = a["b_v"].reshape(2, P).T
    vecs = [chunks(a["g_mix"][0]), chunks(a["g_ffn"][0]), chunks(a["g_ple"][0]), chunks(a["g_kv"]), chunks(a["g_mix"][1]),
            chunks(a["g_ffn"][1]), chunks(a["g_ple"][1]), chunks(a["g_final"]), chunks(a["pool_scale"][0]), bq, bk, bv]
    sk = a["sinks"][0]
    sink = np.zeros((P, 40), sk.dtype)
    for j in range(8):
        for b in range(2):
            sink[:, 5 * j + b] = sink[:, 5 * j + 2 + b] = sk[heads[2 * j + b]]
            sink[64 * b:64 * b + 64, 5 * j + 4] = sk[heads[2 * j + b]]
    ins = {
        "xT": np.concatenate([a["x_prompt"][0], a["x_sample"][0]], 0).T,
        "pT": np.concatenate([a["p_prompt"][:, 0], a["p_sample"][:, 0]], 1).transpose(0, 2, 1),
        "histT": a["state_pool"][0, 0].T,
        "vec": np.stack(vecs, 1),
        "br": a["b_router"].T,
        "sinks": sink,
        "cache_kT": a["cache_k"][0].transpose(1, 2, 0).reshape(256, 128),
        "cache_v": a["cache_v"][0].reshape(128, 256),
        "w_pool": a["w_pool"][0], "w_k": a["w_k"], "w_v": a["w_v"],
        "w_q": a["w_q"][0].reshape(D, 16, 64)[:, heads].reshape(D, D),
        "w_o": a["w_o"][0].reshape(16, 64, D)[heads].reshape(D, D),
        "w1_dense": a["w1_dense"][0], "w3_dense": a["w3_dense"][0], "w2_dense": a["w2_dense"][0],
        "w_router": a["w_router"][0], "w1_moe": a["w1_moe"][0], "w3_moe": a["w3_moe"][0], "w2_moe": a["w2_moe"][0],
        "w_ple_proj": a["w_ple_proj"], "w_ple_gate": a["w_ple_gate"],
    }
    outs = {"yT": (D, T), "poolT_prompt": (D, HIST), "poolT_sample": (D, HIST), "kT_prompt": (256, 128), "kT_sample": (256, 128),
            "v_prompt": (128, 256), "v_sample": (128, 256)}
    nc = bacc.Bacc("TRN2", target_bir_lowering=False, num_devices=1)
    A, arrays = {}, {}
    for name, x in ins.items():
        arrays["in_" + name] = np.ascontiguousarray(x)
        A[name] = nc.dram_tensor("in_" + name, x.shape, mybir.dt.from_np(x.dtype), kind="ExternalInput").ap()
    for name, shape in outs.items():
        A[name] = nc.dram_tensor("out_" + name, shape, F32, kind="ExternalOutput").ap()
    build(nc, A)
    r = run(nc, [arrays], core_ids=[0]).results[0]
    o = {name: np.asarray(r["out_" + name]) for name in outs}
    y = o["yT"].T

    def keys(x):
        return np.ascontiguousarray(x.reshape(4, 64, 128).transpose(2, 0, 1))[None]

    return (np.ascontiguousarray(y[:TP])[None], np.ascontiguousarray(y[TP:])[None],
            np.ascontiguousarray(o["poolT_prompt"].T)[None, None], np.ascontiguousarray(o["poolT_sample"].T)[None, None],
            keys(o["kT_prompt"]), o["v_prompt"].reshape(1, 128, 4, 64), keys(o["kT_sample"]), o["v_sample"].reshape(1, 128, 4, 64))
```
